# Optimizing a Trainium2 kernel written in Bass

```python
import jax, jax.numpy as jnp
from jax import lax
import numpy as np

D_MODEL = 1024
BATCH = 1
SEQ = 256
DEPTH = 4

N_MIXERS = 3
N_LAYERS_A = (DEPTH + 2) // 3
N_LAYERS_B = (DEPTH + 1) // 3
N_LAYERS_C = DEPTH // 3

EPS = 1e-6
NEG = -1e30
FORCE = 1e30
D_FF = 2816
FFN_RESID = 0.5
MOBA_HEADS = 16
MOBA_HEAD_DIM = D_MODEL // MOBA_HEADS
MOBA_BLOCK = 256
MOBA_TOPK = 3
MOBA_Q_CHUNK = 32
LRU_WIDTH = D_MODEL
LRU_BLOCKS = 4
LRU_BLOCK_W = LRU_WIDTH // LRU_BLOCKS
CONV_WIDTH = 4
LRU_C = 8.0
NSA_HEADS = 16
NSA_KV_GROUPS = 4
NSA_HEAD_DIM = 64
NSA_HPG = NSA_HEADS // NSA_KV_GROUPS
NSA_CMP_BLOCK = 32
NSA_CMP_STRIDE = 16
NSA_SEL_BLOCK = 64
NSA_TOPN = 16
NSA_LOCAL_BLOCKS = 2
NSA_WINDOW = 512
NSA_CMP_HIDDEN = 256
NSA_Q_CHUNK = 64
NSA_N_BRANCH = 3
NSA_KV_W = NSA_KV_GROUPS * NSA_HEAD_DIM
NSA_IN_WIDTH = NSA_HEADS * NSA_HEAD_DIM + 6 * NSA_KV_W + NSA_N_BRANCH * NSA_HEADS

kernel_name = "hybrid_moba_rglru_nsa_macaron"

F32 = jnp.float32

def rms_norm(x, g):
    xf = x.astype(F32)
    y = xf * lax.rsqrt(jnp.mean(xf * xf, axis=-1, keepdims=True) + EPS)
    return (y * g.astype(F32)).astype(x.dtype)

def swiglu_ffn(x, w_in, w_out):
    gate, up = jnp.split(x @ w_in, 2, axis=-1)
    return (jax.nn.silu(gate) * up) @ w_out

def moba_mixer(x, w_in, q_gain, k_gain, w_out):
    B, S, _ = x.shape
    H, hd, BS, Qc = MOBA_HEADS, MOBA_HEAD_DIM, MOBA_BLOCK, MOBA_Q_CHUNK
    nb = -(-S // BS)
    s_pad = nb * BS
    n_sel = min(MOBA_TOPK, nb)
    scale = hd ** -0.5
    q, k, v = jnp.split(x @ w_in, 3, axis=-1)
    q = rms_norm(q.reshape(B, S, H, hd), q_gain)
    k = rms_norm(k.reshape(B, S, H, hd), k_gain)
    v = v.reshape(B, S, H, hd)
    pad = ((0, 0), (0, s_pad - S), (0, 0), (0, 0))
    k_blk = jnp.pad(k, pad).reshape(B, nb, BS, H, hd).transpose(0, 3, 1, 2, 4)
    v_blk = jnp.pad(v, pad).reshape(B, nb, BS, H, hd).transpose(0, 3, 1, 2, 4)
    k_mean = jnp.mean(k_blk.astype(F32), axis=3).astype(k.dtype)
    n_chunks = S // Qc
    q_chunks = q.reshape(B, n_chunks, Qc, H, hd).transpose(1, 0, 3, 2, 4)
    b_ix = jnp.arange(B)[:, None, None, None]
    h_ix = jnp.arange(H)[None, :, None, None]
    blk_ids = jnp.arange(nb)

    def attend_chunk(args):
        ci, qc = args
        t0 = ci * Qc
        own = t0 // BS
        pos = t0 + jnp.arange(Qc)
        gate = jnp.einsum('bhqd,bhnd->bhqn', qc, k_mean, preferred_element_type=F32)
        gate = jnp.where(blk_ids < own, gate, NEG)
        _, sel = lax.top_k(gate, n_sel)
        sel_ok = sel < own
        k_sel = k_blk[b_ix, h_ix, sel]
        v_sel = v_blk[b_ix, h_ix, sel]
        k_own = lax.dynamic_index_in_dim(k_blk, own, axis=2, keepdims=False)
        v_own = lax.dynamic_index_in_dim(v_blk, own, axis=2, keepdims=False)
        s_own = jnp.einsum('bhqd,bhkd->bhqk', qc, k_own, preferred_element_type=F32) * scale
        own_mask = (own * BS + jnp.arange(BS))[None, :] <= pos[:, None]
        s_own = jnp.where(own_mask, s_own, NEG)
        s_sel = jnp.einsum('bhqd,bhqnkd->bhqnk', qc, k_sel, preferred_element_type=F32) * scale
        s_sel = jnp.where(sel_ok[..., None], s_sel, NEG).reshape(B, H, Qc, n_sel * BS)
        p = jax.nn.softmax(jnp.concatenate([s_own, s_sel], axis=-1), axis=-1).astype(v_blk.dtype)
        p_own = p[..., :BS]
        p_sel = p[..., BS:].reshape(B, H, Qc, n_sel, BS)
        return (jnp.einsum('bhqk,bhkd->bhqd', p_own, v_own)
                + jnp.einsum('bhqnk,bhqnkd->bhqd', p_sel, v_sel))

    o = lax.map(attend_chunk, (jnp.arange(n_chunks), q_chunks))
    o = o.transpose(1, 0, 3, 2, 4).reshape(B, S, H * hd)
    return o @ w_out

def _linear_recurrence(c1, c2):
    a1, b1 = c1
    a2, b2 = c2
    return a1 * a2, a2 * b1 + b2

def rglru_mixer(x, w_in, conv_w, conv_b, wa, ba, wx, bx, lam, w_out):
    B, S, _ = x.shape
    xb, yb = jnp.split(x @ w_in, 2, axis=-1)
    y = jax.nn.gelu(yb)
    xc = lax.conv_general_dilated(xb, conv_w, window_strides=(1,), padding=[(CONV_WIDTH - 1, 0)],
                                  dimension_numbers=('NWC', 'WIO', 'NWC'),
                                  feature_group_count=LRU_WIDTH) + conv_b
    xblk = xc.reshape(B, S, LRU_BLOCKS, LRU_BLOCK_W)
    r = jax.nn.sigmoid(jnp.einsum('bsnc,ncd->bsnd', xblk, wa).reshape(B, S, LRU_WIDTH) + ba).astype(F32)
    i = jax.nn.sigmoid(jnp.einsum('bsnc,ncd->bsnd', xblk, wx).reshape(B, S, LRU_WIDTH) + bx).astype(F32)
    log_a = -LRU_C * r * jax.nn.softplus(-lam.astype(F32))
    a = jnp.exp(log_a)
    mult = jnp.sqrt(-jnp.expm1(2.0 * log_a))
    mult = jnp.where((jnp.arange(S) == 0)[None, :, None], 1.0, mult)
    b = mult * i * xc.astype(F32)
    _, h = lax.associative_scan(_linear_recurrence, (a, b), axis=1)
    return (h.astype(x.dtype) * y) @ w_out

def nsa_mixer(x, w_in, gate_b, q_gain, kc_gain, ks_gain, kw_gain, pos_k, pos_v,
              ck_w1, ck_w2, cv_w1, cv_w2, w_out):
    B, S, _ = x.shape
    H, G, hpg, hd = NSA_HEADS, NSA_KV_GROUPS, NSA_HPG, NSA_HEAD_DIM
    l, d, ls, W, Qc = NSA_CMP_BLOCK, NSA_CMP_STRIDE, NSA_SEL_BLOCK, NSA_WINDOW, NSA_Q_CHUNK
    scale = hd ** -0.5
    n_cmp = (S - l) // d + 1
    n_slc = S // ls
    n_top = min(NSA_TOPN, n_slc)
    splits = [int(v) for v in np.cumsum([H * hd] + [NSA_KV_W] * 6)]
    q, kc, vc, ks, vs, kw, vw, g = jnp.split(x @ w_in, splits, axis=-1)
    q = rms_norm(q.reshape(B, S, G, hpg, hd), q_gain)
    gates = jax.nn.sigmoid(g + gate_b).reshape(B, S, G, hpg, NSA_N_BRANCH)
    cmp_idx = (jnp.arange(n_cmp) * d)[:, None] + jnp.arange(l)[None, :]

    def compress(t, pos_emb, w1, w2):
        blk = t.reshape(B, S, G, hd)[:, cmp_idx] + pos_emb[None, None, :, None, :]
        blk = blk.transpose(0, 1, 3, 2, 4).reshape(B, n_cmp, G, l * hd)
        return jax.nn.gelu(blk @ w1) @ w2

    k_cmp = rms_norm(compress(kc, pos_k, ck_w1, ck_w2), kc_gain)
    v_cmp = compress(vc, pos_v, cv_w1, cv_w2)
    cmp_end = jnp.arange(n_cmp) * d + l - 1
    c_start = jnp.arange(n_cmp) * d
    s_start = jnp.arange(n_slc) * ls
    overlap = ((c_start[:, None] < s_start[None, :] + ls)
               & (c_start[:, None] + l > s_start[None, :])).astype(F32)
    ks_blk = rms_norm(ks.reshape(B, S, G, hd), ks_gain).reshape(B, n_slc, ls, G, hd).transpose(0, 3, 1, 2, 4)
    vs_blk = vs.reshape(B, n_slc, ls, G, hd).transpose(0, 3, 1, 2, 4)
    wpad = ((0, 0), (W, 0), (0, 0), (0, 0))
    kw_pad = jnp.pad(rms_norm(kw.reshape(B, S, G, hd), kw_gain), wpad)
    vw_pad = jnp.pad(vw.reshape(B, S, G, hd), wpad)
    n_chunks = S // Qc
    q_chunks = q.reshape(B, n_chunks, Qc, G, hpg, hd).transpose(1, 0, 2, 3, 4, 5)
    g_chunks = gates.reshape(B, n_chunks, Qc, G, hpg, NSA_N_BRANCH).transpose(1, 0, 2, 3, 4, 5)
    b_ix = jnp.arange(B)[:, None, None, None]
    g_ix = jnp.arange(G)[None, :, None, None]
    blk_j = jnp.arange(n_slc)

    def attend_chunk(args):
        ci, qc, gc = args
        t0 = ci * Qc
        pos = t0 + jnp.arange(Qc)
        s_c = jnp.einsum('bqghd,bngd->bghqn', qc, k_cmp, preferred_element_type=F32) * scale
        m_c = cmp_end[None, :] <= pos[:, None]
        p_c = jnp.where(m_c, jax.nn.softmax(jnp.where(m_c, s_c, NEG), axis=-1), 0.0)
        o_c = jnp.einsum('bghqn,bngd->bqghd', p_c.astype(v_cmp.dtype), v_cmp)
        imp = jnp.einsum('bghqn,nj->bgqj', p_c, overlap)
        cur = (pos // ls)[:, None]
        forced = (blk_j[None, :] == 0) | ((cur - blk_j[None, :] >= 0) & (cur - blk_j[None, :] < NSA_LOCAL_BLOCKS))
        valid = (blk_j * ls)[None, :] <= pos[:, None]
        imp = jnp.where(valid, jnp.where(forced, FORCE, imp), NEG)
        _, sel = lax.top_k(imp, n_top)
        k_sel = ks_blk[b_ix, g_ix, sel]
        v_sel = vs_blk[b_ix, g_ix, sel]
        kpos = sel[..., None] * ls + jnp.arange(ls)
        m_s = (kpos <= pos[None, None, :, None, None])[:, :, None]
        s_s = jnp.einsum('bqghd,bgqnkd->bghqnk', qc, k_sel, preferred_element_type=F32) * scale
        s_s = jnp.where(m_s, s_s, NEG).reshape(B, G, hpg, Qc, n_top * ls)
        p_s = jax.nn.softmax(s_s, axis=-1).reshape(B, G, hpg, Qc, n_top, ls).astype(v_sel.dtype)
        o_s = jnp.einsum('bghqnk,bgqnkd->bqghd', p_s, v_sel)
        k_w = lax.dynamic_slice_in_dim(kw_pad, t0, W + Qc, axis=1)
        v_w = lax.dynamic_slice_in_dim(vw_pad, t0, W + Qc, axis=1)
        wpos = t0 - W + jnp.arange(W + Qc)
        m_w = ((wpos[None, :] <= pos[:, None]) & (wpos[None, :] > pos[:, None] - W) & (wpos[None, :] >= 0))
        s_w = jnp.einsum('bqghd,bkgd->bghqk', qc, k_w, preferred_element_type=F32) * scale
        p_w = jax.nn.softmax(jnp.where(m_w, s_w, NEG), axis=-1).astype(v_w.dtype)
        o_w = jnp.einsum('bghqk,bkgd->bqghd', p_w, v_w)
        return gc[..., 0:1] * o_c + gc[..., 1:2] * o_s + gc[..., 2:3] * o_w

    o = lax.map(attend_chunk, (jnp.arange(n_chunks), q_chunks, g_chunks))
    o = o.transpose(1, 0, 2, 3, 4, 5).reshape(B, S, H * hd)
    return o @ w_out

def _normal(k, shape, scale):
    return jax.random.normal(k, shape, F32) * scale

def setup_inputs(seed: int = 0) -> dict:
    key = jax.random.key(seed)
    ks = iter(jax.random.split(key, 40))
    D, F = D_MODEL, D_FF
    nA, nB, nC = N_LAYERS_A, N_LAYERS_B, N_LAYERS_C
    Wd, hdA, hdC = LRU_WIDTH, MOBA_HEAD_DIM, NSA_HEAD_DIM
    a0 = jax.random.uniform(next(ks), (nB, Wd), F32, minval=0.9, maxval=0.999)
    s = a0 ** (1.0 / LRU_C)
    return {
        "x": _normal(next(ks), (BATCH, SEQ, D), 1.0),
        "norm_g": 1.0 + _normal(next(ks), (DEPTH, 3, D), 0.01),
        "ffn1_wi": _normal(next(ks), (DEPTH, D, 2 * F), D ** -0.5),
        "ffn1_wo": _normal(next(ks), (DEPTH, F, D), F ** -0.5),
        "ffn2_wi": _normal(next(ks), (DEPTH, D, 2 * F), D ** -0.5),
        "ffn2_wo": _normal(next(ks), (DEPTH, F, D), F ** -0.5),
        "moba_w_in": _normal(next(ks), (nA, D, 3 * MOBA_HEADS * hdA), D ** -0.5),
        "moba_q_gain": 1.0 + _normal(next(ks), (nA, hdA), 0.01),
        "moba_k_gain": 1.0 + _normal(next(ks), (nA, hdA), 0.01),
        "moba_w_out": _normal(next(ks), (nA, MOBA_HEADS * hdA, D), (MOBA_HEADS * hdA) ** -0.5),
        "lru_w_in": _normal(next(ks), (nB, D, 2 * Wd), D ** -0.5),
        "lru_conv_w": _normal(next(ks), (nB, CONV_WIDTH, 1, Wd), CONV_WIDTH ** -0.5),
        "lru_conv_b": _normal(next(ks), (nB, Wd), 0.01),
        "lru_wa": _normal(next(ks), (nB, LRU_BLOCKS, LRU_BLOCK_W, LRU_BLOCK_W), LRU_BLOCK_W ** -0.5),
        "lru_ba": _normal(next(ks), (nB, Wd), 0.01),
        "lru_wx": _normal(next(ks), (nB, LRU_BLOCKS, LRU_BLOCK_W, LRU_BLOCK_W), LRU_BLOCK_W ** -0.5),
        "lru_bx": _normal(next(ks), (nB, Wd), 0.01),
        "lru_lam": jnp.log(s) - jnp.log1p(-s),
        "lru_w_out": _normal(next(ks), (nB, Wd, D), Wd ** -0.5),
        "nsa_w_in": _normal(next(ks), (nC, D, NSA_IN_WIDTH), D ** -0.5),
        "nsa_gate_b": _normal(next(ks), (nC, NSA_N_BRANCH * NSA_HEADS), 0.01),
        "nsa_q_gain": 1.0 + _normal(next(ks), (nC, hdC), 0.01),
        "nsa_kc_gain": 1.0 + _normal(next(ks), (nC, hdC), 0.01),
        "nsa_ks_gain": 1.0 + _normal(next(ks), (nC, hdC), 0.01),
        "nsa_kw_gain": 1.0 + _normal(next(ks), (nC, hdC), 0.01),
        "nsa_pos_k": _normal(next(ks), (nC, NSA_CMP_BLOCK, hdC), 0.1),
        "nsa_pos_v": _normal(next(ks), (nC, NSA_CMP_BLOCK, hdC), 0.1),
        "nsa_ck_w1": _normal(next(ks), (nC, NSA_CMP_BLOCK * hdC, NSA_CMP_HIDDEN), (NSA_CMP_BLOCK * hdC) ** -0.5),
        "nsa_ck_w2": _normal(next(ks), (nC, NSA_CMP_HIDDEN, hdC), NSA_CMP_HIDDEN ** -0.5),
        "nsa_cv_w1": _normal(next(ks), (nC, NSA_CMP_BLOCK * hdC, NSA_CMP_HIDDEN), (NSA_CMP_BLOCK * hdC) ** -0.5),
        "nsa_cv_w2": _normal(next(ks), (nC, NSA_CMP_HIDDEN, hdC), NSA_CMP_HIDDEN ** -0.5),
        "nsa_w_out": _normal(next(ks), (nC, NSA_HEADS * hdC, D), (NSA_HEADS * hdC) ** -0.5),
    }

def reference(x, norm_g, ffn1_wi, ffn1_wo, ffn2_wi, ffn2_wo,
              moba_w_in, moba_q_gain, moba_k_gain, moba_w_out,
              lru_w_in, lru_conv_w, lru_conv_b, lru_wa, lru_ba, lru_wx, lru_bx, lru_lam, lru_w_out,
              nsa_w_in, nsa_gate_b, nsa_q_gain, nsa_kc_gain, nsa_ks_gain, nsa_kw_gain,
              nsa_pos_k, nsa_pos_v, nsa_ck_w1, nsa_ck_w2, nsa_cv_w1, nsa_cv_w2, nsa_w_out):
    h = x
    for i in range(DEPTH):
        j = i // N_MIXERS
        kind = i % N_MIXERS
        h = h + FFN_RESID * swiglu_ffn(rms_norm(h, norm_g[i, 0]), ffn1_wi[i], ffn1_wo[i])
        u = rms_norm(h, norm_g[i, 1])
        if kind == 0:
            m = moba_mixer(u, moba_w_in[j], moba_q_gain[j], moba_k_gain[j], moba_w_out[j])
        elif kind == 1:
            m = rglru_mixer(u, lru_w_in[j], lru_conv_w[j], lru_conv_b[j], lru_wa[j], lru_ba[j],
                            lru_wx[j], lru_bx[j], lru_lam[j], lru_w_out[j])
        else:
            m = nsa_mixer(u, nsa_w_in[j], nsa_gate_b[j], nsa_q_gain[j], nsa_kc_gain[j], nsa_ks_gain[j],
                          nsa_kw_gain[j], nsa_pos_k[j], nsa_pos_v[j], nsa_ck_w1[j], nsa_ck_w2[j],
                          nsa_cv_w1[j], nsa_cv_w2[j], nsa_w_out[j])
        h = h + m
        h = h + FFN_RESID * swiglu_ffn(rms_norm(h, norm_g[i, 2]), ffn2_wi[i], ffn2_wo[i])
    return h


_drawn_inputs = setup_inputs


def setup_inputs(seed=0):
    import zlib

    import numpy as np

    out = dict(_drawn_inputs(seed))
    spreads = {}
    factors = {'norm_g': 3.867,
     'moba_q_gain': 8.0,
     'moba_k_gain': 8.0,
     'lru_ba': 8.0,
     'lru_bx': 8.0,
     'nsa_gate_b': 44.963,
     'nsa_q_gain': 8.0,
     'nsa_kc_gain': 64.0,
     'nsa_ks_gain': 8.0,
     'nsa_kw_gain': 8.0,
     'nsa_pos_k': 7.971,
     'nsa_pos_v': 7.724}
    for name, (base, spread) in spreads.items():
        noise = np.random.default_rng([zlib.crc32(name.encode()), seed]).standard_normal(out[name].shape)
        drawn = base * np.exp(spread * noise) if base else spread * noise
        out[name] = __import__('jax').numpy.asarray(drawn.astype(out[name].dtype))
    for name, factor in factors.items():
        out[name] = (out[name] * factor).astype(out[name].dtype)
    return out
```

```python
from contextlib import ExitStack

import numpy as np

import concourse.bass as bass
from concourse import mybir

F32 = mybir.dt.float32
F32R = mybir.dt.float32r
ALU = mybir.AluOpType
ACT = mybir.ActivationFunctionType
AX = mybir.AxisListType

P = 128
D = 1024
S = 256
DEPTH = 4
FF = 2816
EPS = 1e-6
NEG = -1e30
KD = D // P
NF = FF // P
TT = S // P
RING = 4
BW = 8 * P
HEADS = 16
HD = 64
SCALE = HD ** -0.5
CHUNK = 512
CONV = 4
LRU_C = 8.0
GROUPS = 4
HPG = HEADS // GROUPS
CMP_L, CMP_D = 32, 16
NCMP = (S - CMP_L) // CMP_D + 1
CMP_HID = 256
NPAIR = CMP_L // 2
CN = GROUPS * NCMP
KINDS = ["moba", "lru", "nsa"]


class Stage:

    def __init__(self, kind, n_blocks, n_outs, **more):
        self.kind, self.n_blocks, self.n_outs = kind, n_blocks, n_outs
        self.b0 = self.o0 = 0
        self.w = more.get("w")
        self.mixer, self.j = more.get("mixer"), more.get("j")
        self.norm = more.get("norm")
        self.upd = more.get("upd")
        self.ffn, self.bcast, self.pair = more.get("ffn"), more.get("bcast"), more.get("pair")
        self.y, self.nat, self.branch = more.get("y"), more.get("nat"), more.get("branch")
        self.branches = more.get("branches")
        self.nat_stage = more.get("nat_stage")


def plan(depth):
    stages = []
    ffn = upd = bcast = y = nat = pair = branch = 0

    def add_ffn(layer, which):
        nonlocal ffn, upd, bcast, pair
        norm = 3 * layer + (0 if which == 0 else 2)
        stages.append(Stage("up", 2 * NF, 2 * NF, w=2 * layer + which, ffn=ffn, norm=norm, bcast=bcast, pair=pair))
        pair += NF
        stages.append(Stage("down", 3 * KD, KD, w=2 * layer + which, ffn=ffn, upd=upd))
        ffn, upd, bcast = ffn + 1, upd + 1, bcast + 1

    for layer in range(depth):
        add_ffn(layer, 0)
        kind, j = KINDS[layer % 3], layer // 3
        norm = 3 * layer + 1
        if kind == "moba":
            stages.append(Stage("nat", 24, 12, mixer="moba", j=j, norm=norm, nat=nat, branch=branch, y=y,
                                branches=HEADS))
            nat, branch = nat + 1, branch + HEADS
        elif kind == "nsa":
            stages.append(Stage("nat", 24, 12, mixer="nsa", j=j, norm=norm, nat=nat, branch=branch, y=y,
                                branches=2 * HEADS))
            nat, branch = nat + 1, branch + 2 * HEADS
            stages.append(Stage("compress", 8, 4, mixer="nsa", j=j, pair=pair, nat_stage=stages[-1]))
            pair += 2
        else:
            stages.append(Stage("lru_in", 16, 16, mixer="lru", j=j, norm=norm, bcast=bcast, y=y, pair=pair))
            bcast, y, pair = bcast + 1, y + 8, pair + 8
            stages.append(Stage("gates", 4, 16, mixer="lru", j=j, y=y, pair=pair))
            pair += 8
        stages.append(Stage("out", 8, 8, mixer=kind, j=j, upd=upd, y=y))
        y += 8
        upd += 1
        add_ffn(layer, 1)
    b = o = 0
    for st in stages:
        st.b0, st.o0 = b, o
        b, o = b + st.n_blocks, o + st.n_outs
        assert b % RING == 0 and o % 4 == 0
    return stages, b


class Part:

    def __init__(self, chunk, col, heads, slot, gain):
        self.chunk, self.col, self.heads, self.slot, self.gain = chunk, col, heads, slot, gain


GAIN0 = {("moba", 0): 0, ("nsa", 0): 2, ("moba", 1): 5}
Q_COL = {"moba": 0, "nsa": 512}
KS_COL, VS_COL, KW_COL, VW_COL, G_COL = 1536, 1792, 2048, 2304, 2560
NG = 3 * HEADS
MOBA_V_COL = 2048


def parts_of(mixer, j):
    g = GAIN0[mixer, j]
    if mixer == "moba":
        return [Part(0, 0, 8, 0, g), Part(1, 512, 8, 8, g), Part(2, 1024, 8, 16, g + 1), Part(3, 1536, 8, 24, g + 1)]
    return [Part(1, 512, 8, 0, g), Part(2, 1024, 8, 8, g), Part(3, KS_COL, 4, 16, g + 1), Part(4, KW_COL, 4, 20, g + 2)]


def trunk_program(nc, depth, t):
    stages, n_blocks = plan(depth)
    norms = 3 * depth
    parts = {(st.mixer, st.j): parts_of(st.mixer, st.j) for st in stages if st.kind == "nat"}
    with ExitStack() as ctx:
        def sb(name, shape, dt=F32):
            return ctx.enter_context(nc.sbuf_tensor(name, shape, dt))

        def sem(name):
            return ctx.enter_context(nc.semaphore(name))

        def reach(eng, s, value):
            if not isinstance(value, int) or value > 0:
                eng.wait_ge(s, value)

        raw = sb("raw", [P, RING, BW])
        w_hi = sb("w_hi", [P, RING, BW], F32R)
        w_lo = sb("w_lo", [P, RING, BW], F32R)
        X = sb("X", [P, KD, 2 * S], F32R)
        H = sb("H", [P, NF, 2 * S], F32R)
        h = sb("h", [P, KD, S])
        gains = sb("gains", [P, norms, KD])
        sq = sb("sq", [P, 2, S])
        ssum = sb("ssum", [P, S])
        sd = sb("sd", [P, TT])
        rstd = sb("rstd", [P, TT])
        rdiag = sb("rdiag", [P, TT, P])
        rb = sb("rb", [P, S])
        eps = sb("eps", [P, 1])
        ones = sb("ones", [P, P])
        ident = sb("ident", [P, P])
        tri = sb("tri", [P, 3, P])
        pairbuf = sb("pairbuf", [P, 2, 2, S])
        bt = pairbuf[:, 0]
        pre = pairbuf[:, 1]
        sqh = pairbuf[:, :, :, :].rearrange("p a b c -> p a (b c)")
        gu = sb("gu", [P, 2, S])
        sg = sb("sg", [P, S])
        hf = sb("hf", [P, S])

        scratch = sb("scratch", [P, 12288])
        QKV = scratch[:, 0:6144].rearrange("p (t c) -> p t c", t=TT)
        QKT = scratch[:, 6144:10240].rearrange("p (q s) -> p q s", s=S)
        O = scratch[:, 10240:12288].rearrange("p (t c) -> p t c", t=TT)
        ssh = sb("ssh", [P, TT, 32])
        sdh = sb("sdh", [P, TT, 32])
        rqh = sb("rqh", [P, TT, 32])
        hgain = sb("hgain", [P, 7, HD])
        rings = sb("rings", [P, 6 * 3 * P])
        SM, PR, PT = (rings[:, n * 768:(n + 1) * 768].rearrange("p (a b) -> p a b", a=2)
                      for n in range(3))
        mx = sb("mx", [P, 4, TT])
        nm = sb("nm", [P, 4, TT])
        sums = sb("sums", [P, 4, TT])
        rsum = sb("rsum", [P, 4, TT])
        cf = sb("cf", [P, 4, TT])

        xpad_all = sb("xpad", [P, KD * (S + CONV - 1)])
        xpad = xpad_all[:, :].rearrange("p (k s) -> p k s", s=S + CONV - 1)
        XC, YG, RG, IG, AA, TH = (scratch[:, n * 2048:(n + 1) * 2048].rearrange("p (k s) -> p k s", s=S)
                                  for n in range(6))
        cols = sb("cols", [P, KD, CONV + 4])
        lam = sb("lam", [P, 8, KD])
        loga = sb("loga", [P, KD])

        gbias = sb("gbias", [P, NG])
        G = sb("G", [P, TT, NG])
        pos = sb("pos", [P, 2, NPAIR])
        w2k = sb("w2k", [P, 2, P])
        w2v = sb("w2v", [P, 2, HD])
        kcgain = sb("kcgain", [P, 1])
        x2f = scratch[:, 10240:10240 + 2 * NPAIR * CN].rearrange("p (a m n) -> p a m n", a=2, n=CN)
        X2 = H[:, 8:16, :].rearrange("p f s -> p (f s)")[:, 0:4 * NPAIR * CN].rearrange(
            "p (a m n) -> p a m n", a=2, n=2 * CN)
        hc = sb("hc", [P, 2, 2, CN])
        HV = rings[:, 0:1024].rearrange("p (k g r n) -> p k g r n", k=2, g=GROUPS, r=HPG)
        blk = sb("blk", [P, P])
        sqc = sb("sqc", [P, 3, CN])
        KC = sb("KC", [P, CN])
        VC = sb("VC", [P, GROUPS, HD])
        cmask = sb("cmask", [P, 2, TT, NCMP])
        SC, PCE = (rings[:, o:o + 512].rearrange("p (e t h n) -> p e t h n", e=2, t=TT, h=8) for o in (1024, 1536))
        cst = sb("cst", [P, 4, 2 * TT * 8])
        PC = xpad_all[:, 0:1024].rearrange("p (t h n) -> p t h n", t=TT, h=HEADS)
        KVD = O.rearrange("p t (g e d) -> p t g e d", e=2, d=HD)
        KSD = rings[:, 1024:2048].rearrange("p (t g e d) -> p t g e d", t=TT, e=2, d=HD)
        KWD = xpad_all[:, 1024:2048].rearrange("p (t g e d) -> p t g e d", t=TT, e=2, d=HD)
        PCT = xpad_all[:, 1024:2048].rearrange("p (t c) -> p t c", t=TT)

        PS = ctx.enter_context(nc.psum_tensor("PS", [P, 8, 512], F32))
        STAT, BC = 6, 6

        block_loaded = [sem(f"block_loaded{i}") for i in range(RING)]
        hi_ready, lo_ready, blocks_used = sem("hi_ready"), sem("lo_ready"), sem("blocks_used")
        acc_free, low_copied = sem("acc_free"), sem("low_copied")
        x_loaded, consts_loaded, out_stored = sem("x_loaded"), sem("consts_loaded"), sem("out_stored")
        masks_set, eps_set = sem("masks_set"), sem("eps_set")
        xhi_ready, x_ready = sem("xhi_ready"), sem("x_ready")
        squared, summed = sem("squared"), sem("summed")
        stat_full, sd_ready, rstd_ready = sem("stat_full"), sem("sd_ready"), sem("rstd_ready")
        diag_ready, rb_full, rb_ready = sem("diag_ready"), sem("rb_full"), sem("rb_ready")
        half_added = sem("half_added")
        scaled, silu_ready, prod_ready = sem("scaled"), sem("silu_ready"), sem("prod_ready")
        hhi_ready, h_ready = sem("hhi_ready"), sem("h_ready")
        heads_squared, heads_summed, head_sd, head_rms = (sem("heads_squared"), sem("heads_summed"),
                                                          sem("head_sd"), sem("head_rms"))
        heads_scaled, heads_gained = sem("heads_scaled"), sem("heads_gained")
        turned, turned_act, turned_dve = sem("turned"), sem("turned_act"), sem("turned_dve")
        scores_full, masked, negmax, probs_ready = sem("scores_full"), sem("masked"), sem("negmax"), sem("probs_ready")
        pt_full, pt_ready, o_full, o_done = sem("pt_full"), sem("pt_ready"), sem("o_full"), sem("o_done")
        sum_inv, coef_ready = sem("sum_inv"), sem("coef_ready")
        ot_full, yhi_ready, y_ready = sem("ot_full"), sem("yhi_ready"), sem("y_ready")
        pad_set, lru_scaled, gelu_done = sem("pad_set"), sem("lru_scaled"), sem("gelu_done")
        tap_added, xc_hi, gates_ready = sem("tap_added"), sem("xc_hi"), sem("gates_ready")
        lam_exp, lam_step = sem("lam_exp"), sem("lam_step")
        decay_ready, decay_squared, gated = sem("decay_ready"), sem("decay_squared"), sem("gated")
        mult2_ready, mult_ready, input_ready = sem("mult2_ready"), sem("mult_ready"), sem("input_ready")
        scanned, hy_ready, hy_hi = sem("scanned"), sem("hy_ready"), sem("hy_hi")
        win_turned, win_ready, win_hi, win_low = sem("win_turned"), sem("win_ready"), sem("win_hi"), sem("win_low")
        gate_raw, gate_ready = sem("gate_raw"), sem("gate_ready")
        nsa_zeroed, hidden_ready, hidden_spread = sem("nsa_zeroed"), sem("hidden_ready"), sem("hidden_spread")
        kc_full, kc_squared, kc_summed, kc_sd = sem("kc_full"), sem("kc_squared"), sem("kc_summed"), sem("kc_sd")
        kc_inv, kc_ready, vc_full, vc_ready = sem("kc_inv"), sem("kc_ready"), sem("vc_full"), sem("vc_ready")
        sc_full, sc_step, pce_ready = sem("sc_full"), sem("sc_step"), sem("pce_ready")
        pc_ready, pct_full, pct_ready = sem("pc_ready"), sem("pct_full"), sem("pct_ready")
        oc_full, oc_done = sem("oc_full"), sem("oc_done")

        const_loads = [("hgain", hgain[:, :, :]), ("lru_cols", cols[:, :, :]), ("nsa_gate_b", gbias[:, :]),
                       ("nsa_pos", pos[:, :, :]), ("nsa_w2k", w2k[:, :, :]), ("nsa_w2v", w2v[:, :, :]),
                       ("nsa_kc_gain", kcgain[:, :])]
        CONSTS = len(const_loads)

        block = ctx.enter_context(nc.Block())

        def conv_cols(b):
            for st in stages:
                if st.b0 <= b < st.b0 + st.n_blocks:
                    i = b - st.b0
                    if st.kind == "down" and i % 3 == 2:
                        return (NF - 16) * P
                    if st.kind == "nat" and st.mixer == "nsa" and i >= 20:
                        return 2 * NG
                    return BW

        @block.sync
        def _(sp):
            def load(b, ring, src, n=BW):
                reach(sp, lo_ready, b - RING + 1)
                sp.dma_start(raw[:, ring, 0:n], src).then_inc(block_loaded[ring], 16)

            def down_src(w, d, s):
                n = BW if s < 2 else (NF - 16) * P
                return t["down_w"][w, d][:, s * BW:s * BW + n], n

            sp.dma_start(h[:, :, :], t["x"]).then_inc(x_loaded, 16)
            sp.dma_start(gains[:, :, :], t["norm_g"]).then_inc(x_loaded, 16)
            for st in stages:
                b0 = st.b0
                if st.kind == "up":
                    first = 0
                    if b0 == 0:
                        first = 1
                        for s in range(4):
                            load(s, s, t["up_w"][st.w, s])
                    with sp.Fori(first, 2 * NF // 4) as it:
                        for s in range(4):
                            load(b0 + 4 * it + s, s, t["up_w"][st.w, 4 * it + s])
                elif st.kind == "down":
                    with sp.Fori(0, KD // 4) as it:
                        for d in range(4):
                            for s in range(3):
                                src, n = down_src(st.w, 4 * it + d, s)
                                load(b0 + 12 * it + 3 * d + s, (3 * d + s) % RING, src, n)
                elif st.kind == "nat" and st.mixer == "nsa":
                    with sp.Fori(0, 5) as it:
                        for s in range(4):
                            load(b0 + 4 * it + s, s, t["nsa_w"][st.j, 4 * it + s])
                    for s in range(4):
                        load(b0 + 20 + s, s, t["nsa_g"][st.j, s], 2 * NG)
                else:
                    arr = {"nat": "moba_w", "lru_in": "lru_w", "gates": "lru_g", "compress": "nsa_c",
                           "out": st.mixer + "_o"}[st.kind]
                    with sp.Fori(0, st.n_blocks // 4) as it:
                        for s in range(4):
                            load(b0 + 4 * it + s, s, t[arr][st.j, 4 * it + s])
            last = stages[-1]
            for d in range(KD):
                sp.wait_ge(acc_free, last.o0 + d + 1)
                sp.dma_start(t["out"][:, d, :], h[:, d, :]).then_inc(out_stored, 16)
            sp.wait_ge(out_stored, 16 * KD)

        @block.tensor
        def _(pe):
            mm = nc.tensor.matmul

            def tile(bank, ring, col, rhs, n, first, last):
                mm(PS[:, bank, 0:2 * n], w_hi[:, ring, col:col + P], rhs[:, 0:2 * n], start=first, stop=False,
                   skip_group_check=True)
                return mm(PS[:, bank, 0:n], w_lo[:, ring, col:col + P], rhs[:, 0:n], start=False, stop=last,
                          skip_group_check=True)

            def stats(norm):
                pe.wait_ge(summed, KD * (norm + 1))
                for tt in range(TT):
                    last = mm(PS[:, STAT, tt:tt + 1], ssum[:, tt * P:(tt + 1) * P], ones[:, 0:1], start=True, stop=True)
                last.then_inc(stat_full, 1)

            def spread(nb):
                pe.wait_ge(diag_ready, nb + 1)
                mm(PS[:, BC, 256:512], ones[:, :], rdiag[:, :, :], start=True, stop=True).then_inc(rb_full, 1)

            def pair(st, i, par, rhs_ready=None, peeled=False):
                for g in range(2):
                    b, ring = st.b0 + 2 * i + g, (2 * par + g) % RING
                    pe.wait_ge(lo_ready, b + 1)
                    reach(pe, acc_free, st.o0 + 2 * i + g - 3)
                    for k in range(KD):
                        if peeled and g == 0:
                            pe.wait_ge(x_ready, KD * st.norm + k + 1)
                        last = tile(2 * par + g, ring, k * P, X[:, k, :], S, k == 0, k == KD - 1)
                    last.then_inc(blocks_used, 1)
                    if peeled and i == 0:
                        if g == 0:
                            stats(st.norm)
                        else:
                            spread(st.bcast)

            def up(st):
                n = st.n_outs // 2
                for i in range(2):
                    pair(st, i, i, peeled=(i == 0))
                with nc.tensor.Fori(1, n // 2) as it:
                    for s in range(2):
                        pair(st, 2 * it + s, s)

            def down(st):
                with nc.tensor.Fori(0, KD // 4) as it:
                    for d in range(4):
                        reach(pe, acc_free, st.o0 + 4 * it + d - 3)
                        for s in range(3):
                            b, ring = st.b0 + 12 * it + 3 * d + s, (3 * d + s) % RING
                            pe.wait_ge(lo_ready, b + 1)
                            hi = min(8 * s + 8, NF)
                            pe.wait_ge(h_ready, NF * st.ffn + hi)
                            for f in range(8 * s, hi):
                                last = tile(d, ring, (f - 8 * s) * P, H[:, f, :], S, f == 0, f == NF - 1)
                            last.then_inc(blocks_used, 1)

            def out_proj(st):
                with nc.tensor.Fori(0, KD // 4) as it:
                    for d in range(4):
                        reach(pe, acc_free, st.o0 + 4 * it + d - 3)
                        pe.wait_ge(lo_ready, st.b0 + 4 * it + d + 1)
                        for k in range(KD):
                            if d == 0 and k % 2 == 0:
                                pe.wait_ge(y_ready, st.y + k + 2)
                            last = tile(d, d, k * P, H[:, k, :], S, k == 0, k == KD - 1)
                        last.then_inc(blocks_used, 1)

            def chunk(st, c, par, n=CHUNK):
                pe.wait_ge(acc_free, st.o0 + 2 * c - 2)
                for q in range(4):
                    pe.wait_ge(lo_ready, st.b0 + 4 * c + q + 1)
                    for kk in range(2):
                        k = 2 * q + kk
                        for tt in range(TT):
                            out = PS[:, 2 * par + tt, 0:n]
                            x_hi, x_lo = (X[:, k, o + tt * P:o + (tt + 1) * P] for o in (0, S))
                            hi, lo = (w[:, q, kk * n:(kk + 1) * n] for w in (w_hi, w_lo))
                            mm(out, x_hi, hi, start=(k == 0), stop=False)
                            mm(out, x_hi, lo, start=False, stop=False)
                            last = mm(out, x_lo, hi, start=False, stop=(k == KD - 1))
                    last.then_inc(blocks_used, 1)

            def nat(st):
                stats(st.norm)
                pe.wait_ge(x_ready, KD * (st.norm + 1))
                with nc.tensor.Fori(0, 3 if st.mixer == "moba" else 2) as it:
                    for s in range(2):
                        chunk(st, 2 * it + s, s)
                if st.mixer == "nsa":
                    chunk(st, 4, 0)
                    chunk(st, 5, 1, NG)

            def turn_heads(st):
                if st.mixer == "nsa":
                    pe.wait_ge(win_ready, 8)
                for q in range(8):
                    n = 8 * st.nat + q
                    pe.wait_ge(heads_gained, 8 * st.nat + (4 if q < 4 else 8))
                    if q >= 4:
                        pe.wait_ge((turned_act, turned_dve)[q % 2], 4 * st.nat + (q - 4) // 2 + 1)
                    for i in range(2):
                        tl = 2 * q + i
                        for tt in range(TT):
                            if st.mixer == "moba":
                                src = QKV[:, tt, tl * P:(tl + 1) * P]
                            elif tl < 8:
                                c = Q_COL["nsa"] + tl * P
                                src = QKV[:, tt, c:c + P]
                            else:
                                src = (KSD, KWD)[(tl - 8) // 4][:, tt, tl % 4, :, :].rearrange("p e d -> p (e d)")
                            last = nc.tensor.transpose(PS[:, 4 + q % 4, i * S + tt * P:i * S + (tt + 1) * P],
                                                       src, ident[:, :])
                    last.then_inc(turned, 1)

            def attend(st):
                pe.wait_ge(turned_act, 4 * (st.nat + 1))
                pe.wait_ge(turned_dve, 4 * (st.nat + 1))
                pe.wait_ge(acc_free, st.o0 + st.n_outs + (4 if st.mixer == "nsa" else 0))
                for n in range(st.branches + 2):
                    if n < st.branches:
                        head, kt, _, _ = branch_of(st.mixer, n)
                        a = st.branch + n
                        half = slice((head % 2) * HD, (head % 2) * HD + HD)
                        reach(pe, masked, a - 1)
                        mm(PS[:, 4 + n % 2, 0:P], QKT[half, head // 2, 0:P], QKT[half, kt, 0:P], start=True, stop=True)
                        mm(PS[:, 4 + n % 2, P:3 * P], QKT[half, head // 2, P:2 * P], QKT[half, kt, :],
                           start=True, stop=True).then_inc(scores_full, 1)
                    if 1 <= n <= st.branches:
                        a = st.branch + n - 1
                        pe.wait_ge(probs_ready, a + 1)
                        reach(pe, pt_ready, a - 1)
                        for i in range(3):
                            last = nc.tensor.transpose(PS[:, 6 + (n - 1) % 2, i * P:(i + 1) * P],
                                                       PR[:, (n - 1) % 2, i * P:(i + 1) * P], ident[:, :])
                        last.then_inc(pt_full, 1)
                    if n >= 2:
                        m = n - 2
                        _, _, v, _ = branch_of(st.mixer, m)
                        a = st.branch + m
                        pe.wait_ge(pt_ready, a + 1)
                        reach(pe, o_done, a - 1)
                        pt = PT[:, m % 2, :]
                        mm(PS[:, m % 2, 0:HD], pt[:, 0:P], QKV[:, 0, v:v + HD], start=True, stop=True)
                        mm(PS[:, m % 2, HD:2 * HD], pt[:, P:2 * P], QKV[:, 0, v:v + HD], start=True, stop=False)
                        mm(PS[:, m % 2, HD:2 * HD], pt[:, 2 * P:3 * P], QKV[:, 1, v:v + HD], start=False,
                           stop=True).then_inc(o_full, 1)

            def turn_out(st):
                pe.wait_ge(o_done, st.branch + st.branches)
                for q in range(4):
                    for i in range(2):
                        for tt in range(TT):
                            last = nc.tensor.transpose(PS[:, 4 + q, i * S + tt * P:i * S + (tt + 1) * P],
                                                       O[:, tt, (2 * q + i) * P:(2 * q + i + 1) * P], ident[:, :])
                    last.then_inc(ot_full, 1)

            def turn_windows(st):
                pe.wait_ge(acc_free, st.o0 + 2)
                for kv in range(2):
                    for g in range(GROUPS):
                        for tt in range(TT):
                            c = (g % 2) * S + tt * P
                            last = nc.tensor.transpose(PS[:, 4 + 2 * kv + g // 2, c:c + P],
                                                       KVD[:, tt, kv * GROUPS + g, :, :].rearrange("p e d -> p (e d)"),
                                                       ident[:, :])
                    last.then_inc(win_turned, 1)

            def compress(st):
                for kv in range(2):
                    pe.wait_ge(win_low, kv + 1)
                    for hid in range(2):
                        bank = 2 * kv + hid
                        pe.wait_ge(acc_free, st.o0 + bank - 3)
                        for half in range(2):
                            ring = (2 * bank + half) % RING
                            pe.wait_ge(lo_ready, st.b0 + 2 * bank + half + 1)
                            for m in range(8):
                                n = 8 * half + m
                                last = tile(bank, ring, m * P, X2[:, kv, n, :], CN, n == 0, n == NPAIR - 1)
                            last.then_inc(blocks_used, 1)

            def compressed_kv(st):
                pe.wait_ge(hidden_ready, 1)
                for hid in range(2):
                    last = mm(PS[:, 4, 0:CN], w2k[:, hid, :], hc[:, 0, hid, :], start=(hid == 0), stop=(hid == 1))
                last.then_inc(kc_full, 1)
                pe.wait_ge(hidden_spread, 2)
                for g in range(GROUPS):
                    for hid in range(2):
                        last = mm(PS[:, 7, g * HD:(g + 1) * HD], HV[:, hid, g, :, :], w2v[:, hid, :],
                                  start=(hid == 0), stop=(hid == 1))
                last.then_inc(vc_full, 1)
                pe.wait_ge(kc_squared, 1)
                mm(PS[:, 5, 0:CN], blk[:, :], sqc[:, 0, :], start=True, stop=True).then_inc(kc_summed, 1)

            def compressed_attention(st):
                pe.wait_ge(kc_ready, 1)
                pe.wait_ge(turned_act, 4 * (st.nat + 1))
                pe.wait_ge(turned_dve, 4 * (st.nat + 1))
                for head in range(HEADS):
                    half = slice((head % 2) * HD, (head % 2) * HD + HD)
                    g = head // HPG
                    for tt in range(TT):
                        c = (tt * 8 + head // 2) * 16
                        last = mm(PS[:, 4 + head % 2, c:c + NCMP], QKT[half, head // 2, tt * P:(tt + 1) * P],
                                  KC[half, g * NCMP:(g + 1) * NCMP], start=True, stop=True)
                last.then_inc(sc_full, 1)
                pe.wait_ge(pc_ready, 4)
                pe.wait_ge(vc_ready, 1)
                for tt in range(TT):
                    for g in range(GROUPS):
                        last = nc.tensor.transpose(PS[:, 6 + tt, g * P:(g + 1) * P],
                                                   PC[:, tt, HPG * g:HPG * (g + 1), :], ident[:, :])
                    last.then_inc(pct_full, 1)
                pe.wait_ge(pct_ready, 2)
                pe.wait_ge(acc_free, st.o0 + st.n_outs + 4)
                for tt in range(TT):
                    for g in range(GROUPS):
                        for r in range(HPG):
                            rows = slice(32 * r, 32 * r + 32)
                            c = (tt * GROUPS + g) * HD
                            last = mm(PS[:, r, c:c + HD], PCT[rows, tt, g * P:(g + 1) * P], VC[rows, g, :],
                                      start=True, stop=True)
                last.then_inc(oc_full, 1)
                pe.wait_ge(oc_done, HPG)

            def gates(st):
                for q in range(4):
                    pe.wait_ge(lo_ready, st.b0 + q + 1)
                    pe.wait_ge(y_ready, st.y - 8 + 2 * q + 2)
                    for i in range(2):
                        for g in range(2):
                            bank = 2 * i + g
                            pe.wait_ge(acc_free, st.o0 + 4 * q + bank - 3)
                            for kt in range(2):
                                last = tile(bank, q, (2 * bank + kt) * P, H[:, 2 * q + kt, :], S, kt == 0, kt == 1)
                    last.then_inc(blocks_used, 1)

            pe.wait_ge(masks_set, MASKS)
            for st in stages:
                if st.kind in ("up", "lru_in"):
                    up(st)
                elif st.kind == "down":
                    down(st)
                elif st.kind == "out":
                    out_proj(st)
                elif st.kind == "nat":
                    nat(st)
                    if st.mixer == "moba":
                        turn_heads(st)
                        attend(st)
                        turn_out(st)
                elif st.kind == "gates":
                    gates(st)
                elif st.kind == "compress":
                    turn_windows(st.nat_stage)
                    turn_heads(st.nat_stage)
                    compress(st)
                    compressed_kv(st)
                    compressed_attention(st.nat_stage)
                    attend(st.nat_stage)
                    turn_out(st.nat_stage)

        @block.scalar
        def _(act):
            def split(b, ring, n=None, loaded=None):
                if isinstance(b, int):
                    if b >= n_blocks:
                        return
                    n, loaded = conv_cols(b), b // RING + 1
                act.wait_ge(block_loaded[ring], 16 * loaded)
                reach(act, blocks_used, b - RING + 1)
                nc.scalar.copy(w_hi[:, ring, 0:n], raw[:, ring, 0:n]).then_inc(hi_ready, 1)

            def square_and_round(norm, d):
                if norm * KD + d >= 2:
                    act.wait_ge(summed, norm * KD + d - 1)
                nc.scalar.activation(sq[:, d % 2, :], h[:, d, :], ACT.Square).then_inc(squared, 1)
                nc.scalar.activation(X[:, d, 0:S], h[:, d, :], ACT.Copy,
                                     scale=gains[:, norm, d:d + 1]).then_inc(xhi_ready, 1)

            def stats(norm):
                act.wait_ge(stat_full, norm + 1)
                nc.scalar.activation(sd[:, :], PS[:, STAT, 0:TT], ACT.Sqrt, scale=1.0 / D,
                                     bias=eps[:, 0:1]).then_inc(sd_ready, 1)

            def copy_low(st, i, par, used):
                act.wait_ge(blocks_used, used)
                nc.scalar.copy(bt[:, :, :], PS[:, 2 * par:2 * par + 2, S:2 * S]).then_inc(low_copied, 1)

            def round_hidden(st, i):
                act.wait_ge(prod_ready, NF * st.ffn + i + 1)
                nc.scalar.copy(H[:, i, 0:S], hf[:, :]).then_inc(hhi_ready, 1)

            def up_step(st, i, par, it=None, first=False):
                b = st.b0 + 2 * i
                dyn = dict(n=BW, loaded=it) if it is not None else {}
                split(b + 4, 2 * par, **dyn)
                if first:
                    stats(st.norm)
                copy_low(st, i, par, b + 2)
                if not first:
                    round_hidden(st, i - 1)
                split(b + 5, 2 * par + 1, **dyn)
                act.wait_ge(scaled, NF * st.ffn + i + 1)
                nc.scalar.activation(sg[:, :], gu[:, 0, :], ACT.Silu).then_inc(silu_ready, 1)

            def up(st):
                up_step(st, 0, 0, first=True)
                up_step(st, 1, 1)
                with nc.scalar.Fori(1, NF // 2 - 1) as it:
                    for s in range(2):
                        up_step(st, 2 * it + s, s, it=st.b0 // RING + it + 2)
                for i in (NF - 2, NF - 1):
                    up_step(st, i, i % 2)
                round_hidden(st, NF - 1)

            def down(st):
                for d in range(KD):
                    b = st.b0 + 3 * d + 4
                    split(b, b % RING)
                    split(b + 1, (b + 1) % RING)
                    if st.upd + 1 < norms:
                        act.wait_ge(acc_free, st.o0 + d + 1)
                        square_and_round(st.upd + 1, d)
                    split(b + 2, (b + 2) % RING)

            def out_proj(st):
                for d in range(KD):
                    act.wait_ge(acc_free, st.o0 + d + 1)
                    square_and_round(st.upd + 1, d)
                    b = st.b0 + d + 4
                    split(b, b % RING)

            def nat(st):
                last_part = parts[st.mixer, st.j][-1].chunk
                for c in range(6):
                    n = NG if st.mixer == "nsa" and c == 5 else CHUNK
                    if c == 0:
                        stats(st.norm)
                    for q in range(4):
                        split(st.b0 + 4 * c + 4 + q, q)
                    if c == 0:
                        act.wait_ge(rstd_ready, st.norm + 1)
                    if n == NG:
                        continue
                    act.wait_ge(blocks_used, st.b0 + 4 * c + 4)
                    for tt in range(TT):
                        if st.mixer == "nsa" and c == 0:
                            src = PS[:, tt, :].rearrange("p (g d) -> p g d", d=HD).unsqueeze(2).to_broadcast([P, 8, 2, HD])
                            nc.scalar.activation(KVD[:, tt, :, :, :], src, ACT.Copy,
                                                 scale=rstd[:, tt:tt + 1]).then_inc(acc_free, 1)
                            continue
                        nc.scalar.activation(QKV[:, tt, c * CHUNK:c * CHUNK + n], PS[:, 2 * (c % 2) + tt, 0:n],
                                             ACT.Copy, scale=rstd[:, tt:tt + 1]).then_inc(acc_free, 1)
                    if c == last_part + 1:
                        head_norm(st)
                if st.mixer == "nsa":
                    head_norm(st)

            def head_norm(st):
                act.wait_ge(heads_summed, 8 * (st.nat + 1))
                nh = 32 if st.mixer == "moba" else 24
                nc.scalar.activation(sdh[:, :, 0:nh], ssh[:, :, 0:nh], ACT.Sqrt, scale=1.0 / HD,
                                     bias=eps[:, 0:1]).then_inc(head_sd, 1)

            def turn_heads(st):
                for q in range(0, 8, 2):
                    act.wait_ge(turned, 8 * st.nat + q + 1)
                    nc.scalar.copy(QKT[:, 2 * q:2 * q + 2, :], PS[:, 4 + q % 4, :].rearrange("p (a s) -> p a s", a=2)
                                   ).then_inc(turned_act, 1)

            def attend(st):
                for n in range(st.branches + 1):
                    if n < st.branches:
                        a = st.branch + n
                        act.wait_ge(negmax, a + 1)
                        reach(act, pt_full, a - 1)
                        sm, pr = SM[:, n % 2, :], PR[:, n % 2, :]
                        nc.scalar.activation(pr[:, 0:P], sm[:, 0:P], ACT.Exp, scale=SCALE, bias=nm[:, n % 4, 0:1],
                                             accum_out=sums[:, n % 4, 0:1])
                        nc.scalar.activation(pr[:, P:3 * P], sm[:, P:3 * P], ACT.Exp, scale=SCALE,
                                             bias=nm[:, n % 4, 1:2],
                                             accum_out=sums[:, n % 4, 1:2]).then_inc(probs_ready, 1)
                    if n >= 1:
                        m, a = n - 1, st.branch + n - 1
                        act.wait_ge(pt_full, a + 1)
                        reach(act, o_full, a - 1)
                        nc.scalar.copy(PT[:, m % 2, :], PS[:, 6 + m % 2, 0:3 * P]).then_inc(pt_ready, 1)

            def turn_out(st):
                for q in range(4):
                    act.wait_ge(ot_full, 4 * st.nat + q + 1)
                    nc.scalar.copy(H[:, 2 * q:2 * q + 2, 0:S], PS[:, 4 + q, :].rearrange("p (a s) -> p a s", a=2)
                                   ).then_inc(yhi_ready, 1)

            def gates_nsa(st):
                for tt in range(TT):
                    act.wait_ge(gate_raw, tt + 1)
                nc.scalar.activation(G[:, :, :], G[:, :, :], ACT.Sigmoid).then_inc(gate_ready, 1)

            def round_windows():
                for kv in range(2):
                    act.wait_ge(win_ready, 4 * kv + 4)
                    nc.scalar.copy(X2[:, kv, :, 0:CN], x2f[:, kv, :, :]).then_inc(win_hi, 1)

            def compress(st):
                for kv in range(2):
                    for q in range(4):
                        b = st.b0 + 4 + 4 * kv + q
                        split(b, b % RING)
                    act.wait_ge(blocks_used, st.b0 + 4 * kv + 4)
                    nc.scalar.copy(bt[:, :, 0:CN], PS[:, 2 * kv:2 * kv + 2, CN:2 * CN]).then_inc(low_copied, 1)
                    act.wait_ge(acc_free, st.o0 + 2 * kv + 2)
                    nc.scalar.activation(hc[:, kv, :, :], pre[:, :, 0:CN], ACT.Gelu_apprx_tanh).then_inc(hidden_ready, 1)

            def compressed_kv(st):
                act.wait_ge(kc_full, 1)
                nc.scalar.activation(sqc[:, 0, :], PS[:, 4, 0:CN], ACT.Square).then_inc(kc_squared, 1)
                act.wait_ge(vc_full, 1)
                nc.scalar.copy(VC[:, :, :], PS[:, 7, 0:GROUPS * HD].rearrange("p (g d) -> p g d", g=GROUPS)
                               ).then_inc(vc_ready, 1)
                act.wait_ge(kc_summed, 1)
                nc.scalar.activation(sqc[:, 1, :], PS[:, 5, 0:CN], ACT.Sqrt, scale=1.0 / HD,
                                     bias=eps[:, 0:1]).then_inc(kc_sd, 1)

            def compressed_attention(st):
                act.wait_ge(sc_step, 4)
                nc.scalar.activation(PCE[:, :, :, :, 0:NCMP].rearrange("p e t h n -> p (e t h) n"),
                                     SC[:, :, :, :, 0:NCMP].rearrange("p e t h n -> p (e t h) n"),
                                     ACT.Exp, scale=SCALE).then_inc(pce_ready, 1)
                for tt in range(TT):
                    act.wait_ge(pct_full, tt + 1)
                    nc.scalar.copy(PCT[:, tt, :], PS[:, 6 + tt, :]).then_inc(pct_ready, 1)

            def lru_in(st):
                act.wait_ge(consts_loaded, CONSTS * 16)
                nc.scalar.activation(lam[:, 0, :], cols[:, :, LAM], ACT.Abs).then_inc(lam_exp, 1)
                act.wait_ge(lam_exp, 1)
                nc.scalar.activation(lam[:, 1, :], lam[:, 0, :], ACT.Exp, scale=-1.0).then_inc(lam_exp, 1)
                for i in range(KD + 1):
                    if i < KD:
                        par, b = i % 2, st.b0 + 2 * i
                        split(b + 4, 2 * par)
                        if i == 0:
                            stats(st.norm)
                        copy_low(st, i, par, b + 2)
                        split(b + 5, 2 * par + 1)
                        act.wait_ge(lru_scaled, i + 1)
                        nc.scalar.activation(YG[:, i, :], gu[:, 1, :], ACT.Gelu_apprx_tanh).then_inc(gelu_done, 1)
                    if i >= 1:
                        act.wait_ge(tap_added, CONV * i)
                        nc.scalar.copy(H[:, i - 1, 0:S], XC[:, i - 1, :]).then_inc(xc_hi, 1)

            def gates(st):
                for i in range(KD):
                    if i % 2 == 0:
                        b = st.b0 + 4 + i // 2
                        split(b, b % RING)
                    copy_low(st, i, i % 2, st.b0 + i // 2 + 1)
                    act.wait_ge(acc_free, st.o0 + 2 * i + 2)
                    nc.scalar.activation(RG[:, i, :], pre[:, 0, :], ACT.Sigmoid, bias=cols[:, i, BA:BA + 1])
                    nc.scalar.activation(IG[:, i, :], pre[:, 1, :], ACT.Sigmoid,
                                         bias=cols[:, i, BX:BX + 1]).then_inc(gates_ready, 1)
                act.wait_ge(lam_step, LAM_STEPS)
                act.wait_ge(gates_ready, KD)
                for i in range(KD):
                    nc.scalar.activation(AA[:, i, :], RG[:, i, :], ACT.Exp, scale=loga[:, i:i + 1])
                    nc.scalar.activation(TH[:, i, :], RG[:, i, :], ACT.Tanh,
                                         scale=loga[:, i:i + 1]).then_inc(decay_ready, 1)
                for i in range(KD):
                    act.wait_ge(mult2_ready, i + 1)
                    nc.scalar.activation(RG[:, i, :], TH[:, i, :], ACT.Sqrt, scale=-1.0).then_inc(mult_ready, 1)
                for i in range(KD):
                    act.wait_ge(hy_ready, i + 1)
                    nc.scalar.copy(H[:, i, 0:S], TH[:, i, :]).then_inc(hy_hi, 1)

            for b in range(RING):
                split(b, b)
            act.wait_ge(x_loaded, 32)
            act.wait_ge(eps_set, 1)
            for d in range(KD):
                square_and_round(0, d)
            for st in stages:
                if st.kind == "up":
                    up(st)
                elif st.kind == "down":
                    down(st)
                elif st.kind == "out":
                    out_proj(st)
                elif st.kind == "nat":
                    nat(st)
                    if st.mixer == "moba":
                        turn_heads(st)
                        attend(st)
                        turn_out(st)
                elif st.kind == "lru_in":
                    lru_in(st)
                elif st.kind == "gates":
                    gates(st)
                elif st.kind == "compress":
                    round_windows()
                    turn_heads(st.nat_stage)
                    compress(st)
                    compressed_kv(st)
                    gates_nsa(st)
                    compressed_attention(st.nat_stage)
                    attend(st.nat_stage)
                    turn_out(st.nat_stage)

        @block.vector
        def _(dve):
            def split(b, ring, n=None):
                if isinstance(b, int):
                    if b >= n_blocks:
                        return
                    n = conv_cols(b)
                dve.wait_ge(hi_ready, b + 1)
                nc.vector.tensor_tensor(w_lo[:, ring, 0:n], raw[:, ring, 0:n], w_hi[:, ring, 0:n].bitcast(F32),
                                        ALU.subtract).then_inc(lo_ready, 1)

            def low_x(norm, d):
                dve.wait_ge(xhi_ready, norm * KD + d + 1)
                nc.vector.scalar_tensor_tensor(out=X[:, d, S:2 * S], in0=h[:, d, :], scalar=gains[:, norm, d:d + 1],
                                               in1=X[:, d, 0:S].bitcast(F32), op0=ALU.mult, op1=ALU.subtract
                                               ).then_inc(x_ready, 1)

            def update(st, d, used, c):
                dve.wait_ge(blocks_used, used)
                o, bank = st.o0 + d, d % 4
                nc.vector.scalar_tensor_tensor(out=h[:, d, :], in0=PS[:, bank, S:2 * S], scalar=c, in1=h[:, d, :],
                                               op0=ALU.mult, op1=ALU.add).then_inc(half_added, 1)
                dve.wait_ge(half_added, KD * st.upd + d + 1)
                nc.vector.scalar_tensor_tensor(out=h[:, d, :], in0=PS[:, bank, 0:S], scalar=c, in1=h[:, d, :],
                                               op0=ALU.mult, op1=ALU.add).then_inc(acc_free, 1)

            def stats(norm, nb=None):
                dve.wait_ge(sd_ready, norm + 1)
                nc.vector.reciprocal(rstd[:, :], sd[:, :]).then_inc(rstd_ready, 1)
                if nb is not None:
                    dve.wait_ge(rstd_ready, norm + 1)
                    nc.vector.tensor_tensor(rdiag[:, :, :], ident[:, :].unsqueeze(1).to_broadcast([P, TT, P]),
                                            rstd[:, :].unsqueeze(2).to_broadcast([P, TT, P]),
                                            ALU.mult).then_inc(diag_ready, 1)

            def spread(nb):
                dve.wait_ge(rb_full, nb + 1)
                nc.vector.tensor_copy(rb[:, :], PS[:, BC, 256:512]).then_inc(rb_ready, 1)

            def add_low(st, i, par):
                dve.wait_ge(low_copied, st.pair + i + 1)
                nc.vector.tensor_tensor(pre[:, :, :], PS[:, 2 * par:2 * par + 2, 0:S], bt[:, :, :],
                                        ALU.add).then_inc(acc_free, 2)

            def low_hidden(st, i):
                dve.wait_ge(hhi_ready, NF * st.ffn + i + 1)
                nc.vector.tensor_tensor(H[:, i, S:2 * S], hf[:, :], H[:, i, 0:S].bitcast(F32),
                                        ALU.subtract).then_inc(h_ready, 1)

            def up_step(st, i, par, dyn=False, first=False):
                b = st.b0 + 2 * i
                n = dict(n=BW) if dyn else {}
                split(b + 4, 2 * par, **n)
                if first:
                    stats(st.norm, st.bcast)
                add_low(st, i, par)
                if not first:
                    low_hidden(st, i - 1)
                split(b + 5, 2 * par + 1, **n)
                if first:
                    spread(st.bcast)
                dve.wait_ge(silu_ready, NF * st.ffn + i + 1)
                if not first:
                    dve.wait_ge(h_ready, NF * st.ffn + i)
                nc.vector.tensor_tensor(hf[:, :], sg[:, :], gu[:, 1, :], ALU.mult).then_inc(prod_ready, 1)

            def up(st):
                up_step(st, 0, 0, first=True)
                up_step(st, 1, 1)
                with nc.vector.Fori(1, NF // 2 - 1) as it:
                    for s in range(2):
                        up_step(st, 2 * it + s, s, dyn=True)
                for i in (NF - 2, NF - 1):
                    up_step(st, i, i % 2)
                low_hidden(st, NF - 1)

            def down(st):
                for d in range(KD):
                    b = st.b0 + 3 * d + 4
                    split(b, b % RING)
                    split(b + 1, (b + 1) % RING)
                    update(st, d, st.b0 + 3 * d + 3, 0.5)
                    if st.upd + 1 < norms:
                        low_x(st.upd + 1, d)
                    split(b + 2, (b + 2) % RING)

            def out_proj(st):
                for d in range(KD):
                    update(st, d, st.b0 + d + 1, 1.0)
                    low_x(st.upd + 1, d)
                    b = st.b0 + d + 4
                    split(b, b % RING)

            def nat(st):
                ps = parts[st.mixer, st.j]
                n = 8 * st.nat
                for c in range(6):
                    if c == 0:
                        stats(st.norm)
                    for q in range(4):
                        split(st.b0 + 4 * c + 4 + q, q)
                    for part in ps:
                        if part.chunk == c - 1:
                            for tt in range(TT):
                                n += 1
                                dve.wait_ge(heads_squared, n)
                                nc.vector.tensor_reduce(
                                    ssh[:, tt, part.slot:part.slot + part.heads],
                                    sqh[:, n % 2, 0:part.heads * HD].rearrange("p (a b) -> p a b", b=HD),
                                    AX.X, ALU.add).then_inc(heads_summed, 1)
                if st.mixer == "nsa":
                    nsa_gate(st)
                nh = 32 if st.mixer == "moba" else 24
                dve.wait_ge(head_sd, st.nat + 1)
                nc.vector.reciprocal(rqh[:, :, 0:nh], sdh[:, :, 0:nh]).then_inc(head_rms, 1)
                dve.wait_ge(head_rms, st.nat + 1)
                for part in ps:
                    for tt in range(TT):
                        x = QKV[:, tt, part.col:part.col + part.heads * HD].rearrange("p (a b) -> p a b", b=HD)
                        r = rqh[:, tt, part.slot:part.slot + part.heads].unsqueeze(2).to_broadcast([P, part.heads, HD])
                        nc.vector.tensor_tensor(x, x, r, ALU.mult).then_inc(heads_scaled, 1)

            def turn_heads(st):
                for q in range(1, 8, 2):
                    dve.wait_ge(turned, 8 * st.nat + q + 1)
                    nc.vector.tensor_copy(QKT[:, 2 * q:2 * q + 2, :],
                                          PS[:, 4 + q % 4, :].rearrange("p (a s) -> p a s", a=2)
                                          ).then_inc(turned_dve, 1)

            def attend(st):
                for n in range(st.branches + 2):
                    if n < st.branches:
                        a = st.branch + n
                        s = PS[:, 4 + n % 2, :]
                        dve.wait_ge(scores_full, a + 1)
                        reach(dve, probs_ready, a - 1)
                        nc.vector.tensor_tensor_reduce(SM[:, n % 2, 0:P], s[:, 0:P], tri[:, 0, :], 1.0, -3e38,
                                                       ALU.add, ALU.max, mx[:, n % 4, 0:1])
                        nc.vector.tensor_tensor_reduce(SM[:, n % 2, P:3 * P], s[:, P:3 * P],
                                                       tri[:, 1:3, :].rearrange("p a b -> p (a b)"), 1.0, -3e38,
                                                       ALU.add, ALU.max, mx[:, n % 4, 1:2]).then_inc(masked, 1)
                        dve.wait_ge(masked, a + 1)
                        nc.vector.tensor_scalar(nm[:, n % 4, :], mx[:, n % 4, :], -SCALE, None,
                                                ALU.mult).then_inc(negmax, 1)
                    if 1 <= n <= st.branches:
                        m, a = n - 1, st.branch + n - 1
                        dve.wait_ge(probs_ready, a + 1)
                        nc.vector.reciprocal(rsum[:, m % 4, :], sums[:, m % 4, :]).then_inc(sum_inv, 1)
                        head, _, _, gate = branch_of(st.mixer, m)
                        if gate is not None:
                            dve.wait_ge(sum_inv, a + 1)
                            nc.vector.tensor_tensor(cf[:, m % 4, :], rsum[:, m % 4, :], G[:, :, 3 * head + gate],
                                                    ALU.mult).then_inc(coef_ready, 1)
                    if n >= 2:
                        m, a = n - 2, st.branch + n - 2
                        head, _, _, gate = branch_of(st.mixer, m)
                        dve.wait_ge(o_full, a + 1)
                        dve.wait_ge(sum_inv, a + 1)
                        ps = PS[:, m % 2, 0:2 * HD].rearrange("p (t d) -> p t d", t=TT)
                        if gate is None:
                            nc.vector.tensor_tensor(O[:, :, head * HD:(head + 1) * HD], ps,
                                                    rsum[:, m % 4, :].unsqueeze(2).to_broadcast([P, TT, HD]),
                                                    ALU.mult).then_inc(o_done, 1)
                        else:
                            dve.wait_ge(coef_ready, m + 1)
                            reach(dve, o_done, a - HEADS + 1)
                            for tt in range(TT):
                                out = O[:, tt, head * HD:(head + 1) * HD]
                                last = nc.vector.scalar_tensor_tensor(out=out, in0=ps[:, tt, :],
                                                                      scalar=cf[:, m % 4, tt:tt + 1], in1=out,
                                                                      op0=ALU.mult, op1=ALU.add)
                            last.then_inc(o_done, 1)

            def turn_out(st):
                for q in range(4):
                    dve.wait_ge(yhi_ready, 4 * st.nat + q + 1)
                    nc.vector.tensor_tensor(H[:, 2 * q:2 * q + 2, S:2 * S],
                                            PS[:, 4 + q, :].rearrange("p (a s) -> p a s", a=2),
                                            H[:, 2 * q:2 * q + 2, 0:S].bitcast(F32), ALU.subtract).then_inc(y_ready, 2)

            def nsa_gate(st):
                for tt in range(TT):
                    dve.wait_ge(blocks_used, st.b0 + st.n_blocks)
                    dve.wait_ge(acc_free, st.o0 + 10 + tt)
                    nc.vector.scalar_tensor_tensor(out=G[:, tt, :], in0=PS[:, 2 + tt, 0:NG], scalar=rstd[:, tt:tt + 1],
                                                   in1=gbias[:, :], op0=ALU.mult, op1=ALU.add).then_inc(acc_free, 1)
                    dve.wait_ge(acc_free, st.o0 + 11 + tt)
                    nc.vector.tensor_copy(G[:, tt, 0:1], G[:, tt, 0:1]).then_inc(gate_raw, 1)

            def windows():
                dve.wait_ge(consts_loaded, 16 * CONSTS)
                dve.wait_ge(win_turned, 2)
                for kv in range(2):
                    for half in range(2):
                        rows = slice(half * HD, half * HD + HD)
                        v = PS[rows, 4 + 2 * kv:6 + 2 * kv, :].rearrange("p b (g n m e) -> p e m (b g) n", g=2, m=8, e=2)
                        for late in range(2):
                            src = v[:, half, :, :, late:late + NCMP]
                            dst = x2f[rows, kv, 8 * late:8 * late + 8, :].rearrange("p m (g n) -> p m g n", g=GROUPS)
                            add = pos[rows, kv, 8 * late:8 * late + 8].unsqueeze(2).unsqueeze(3).to_broadcast(
                                [HD, 8, GROUPS, NCMP])
                            nc.vector.tensor_tensor(dst, src, add, ALU.add).then_inc(win_ready, 1)
                for kv in range(2):
                    dve.wait_ge(win_hi, kv + 1)
                    nc.vector.tensor_tensor(X2[:, kv, :, CN:2 * CN], x2f[:, kv, :, :],
                                            X2[:, kv, :, 0:CN].bitcast(F32), ALU.subtract).then_inc(win_low, 1)

            def compress(st):
                for kv in range(2):
                    for q in range(4):
                        b = st.b0 + 4 + 4 * kv + q
                        split(b, b % RING)
                    dve.wait_ge(low_copied, st.pair + kv + 1)
                    reach(dve, hidden_ready, kv)
                    nc.vector.tensor_tensor(pre[:, :, 0:CN], PS[:, 2 * kv:2 * kv + 2, 0:CN], bt[:, :, 0:CN],
                                            ALU.add).then_inc(acc_free, 2)

            def compressed_kv(st):
                dve.wait_ge(kc_sd, 1)
                nc.vector.reciprocal(sqc[:, 2, :], sqc[:, 1, :]).then_inc(kc_inv, 1)
                dve.wait_ge(kc_inv, 1)
                nc.vector.scalar_tensor_tensor(out=KC[:, :], in0=PS[:, 4, 0:CN], scalar=kcgain[:, 0:1],
                                               in1=sqc[:, 2, :], op0=ALU.mult, op1=ALU.mult).then_inc(kc_ready, 1)

            def compressed_attention(st):
                dve.wait_ge(sc_full, 1)
                merged = (lambda x: x[:, :, :, :, 0:NCMP].rearrange("p e t h n -> p (e t h) n"))
                wide = [P, 2 * TT * 8, NCMP]
                for e in range(2):
                    ps = PS[:, 4 + e, 0:256].rearrange("p (t h n) -> p t h n", t=TT, h=8)[:, :, :, 0:NCMP]
                    nc.vector.tensor_tensor(SC[:, e, :, :, 0:NCMP], ps,
                                            cmask[:, 0, :, :].unsqueeze(2).to_broadcast([P, TT, 8, NCMP]),
                                            ALU.add).then_inc(sc_step, 1)
                dve.wait_ge(sc_step, 2)
                nc.vector.tensor_reduce(cst[:, 0, :], merged(SC), AX.X, ALU.max).then_inc(sc_step, 1)
                dve.wait_ge(sc_step, 3)
                nc.vector.tensor_tensor(merged(SC), merged(SC), cst[:, 0, :].unsqueeze(2).to_broadcast(wide),
                                        ALU.subtract).then_inc(sc_step, 1)
                dve.wait_ge(pce_ready, 1)
                nc.vector.tensor_reduce(cst[:, 1, :], merged(PCE), AX.X, ALU.add).then_inc(sc_step, 1)
                dve.wait_ge(sc_step, 5)
                nc.vector.reciprocal(cst[:, 2, :], cst[:, 1, :]).then_inc(sc_step, 1)
                dve.wait_ge(sc_step, 6)
                dve.wait_ge(gate_ready, 1)
                nc.vector.tensor_tensor(cst[:, 3, :].rearrange("p (e t h) -> p e t h", e=2, t=TT),
                                        cst[:, 2, :].rearrange("p (e t h) -> p e t h", e=2, t=TT),
                                        G[:, :, :].rearrange("p t (h e b) -> p b e t h", e=2, b=3)[:, 0, :, :, :],
                                        ALU.mult).then_inc(sc_step, 1)
                dve.wait_ge(sc_step, 7)
                nc.vector.tensor_tensor(merged(SC), merged(PCE), cst[:, 3, :].unsqueeze(2).to_broadcast(wide),
                                        ALU.mult).then_inc(sc_step, 1)
                dve.wait_ge(sc_step, 8)
                dve.wait_ge(nsa_zeroed, 2)
                for e in range(2):
                    for tt in range(TT):
                        dst = PC[:, tt, :, 0:NCMP].rearrange("p (h e) n -> p e h n", e=2)[:, e, :, :]
                        nc.vector.tensor_tensor(dst, SC[:, e, tt, :, 0:NCMP],
                                                cmask[:, 1, tt, :].unsqueeze(1).to_broadcast([P, 8, NCMP]),
                                                ALU.mult).then_inc(pc_ready, 1)
                dve.wait_ge(oc_full, 1)
                for r in range(HPG):
                    dst = O[:, :, :].rearrange("p t (g r d) -> p r t g d", g=GROUPS, r=HPG)[:, r, :, :, :]
                    nc.vector.tensor_copy(dst, PS[:, r, :].rearrange("p (t g d) -> p t g d", t=TT, g=GROUPS)
                                          ).then_inc(oc_done, 1)

            def softplus():
                def step(ins):
                    step.n += 1
                    ins.then_inc(lam_step, 1)
                    dve.wait_ge(lam_step, step.n)
                step.n = 0
                u, z, z2, p, m, r = (lam[:, n, :] for n in range(1, 7))
                v = nc.vector
                dve.wait_ge(consts_loaded, CONSTS * 16)
                dve.wait_ge(lam_exp, 2)
                step(v.tensor_scalar(m, cols[:, :, LAM], -1.0, 0.0, ALU.mult, ALU.max))
                step(v.tensor_scalar(z2, u, 2.0, None, ALU.add))
                step(v.reciprocal(r, z2))
                step(v.tensor_tensor(z, u, r, ALU.mult))
                step(v.tensor_tensor(z2, z, z, ALU.mult))
                step(v.tensor_scalar(p, z2, 1.0 / 15, None, ALU.mult))
                for n in (13, 11, 9, 7, 5, 3):
                    step(v.scalar_tensor_tensor(out=p, in0=p, scalar=1.0 / n, in1=z2, op0=ALU.add, op1=ALU.mult))
                step(v.scalar_tensor_tensor(out=p, in0=p, scalar=1.0, in1=z, op0=ALU.add, op1=ALU.mult))
                step(v.scalar_tensor_tensor(out=p, in0=p, scalar=2.0, in1=m, op0=ALU.mult, op1=ALU.add))
                step(v.tensor_scalar(loga[:, :], p, -LRU_C, None, ALU.mult))
                assert step.n == LAM_STEPS

            def lru_in(st):
                softplus()
                for i in range(KD + 1):
                    if i < KD:
                        par, b = i % 2, st.b0 + 2 * i
                        split(b + 4, 2 * par)
                        if i == 0:
                            stats(st.norm, st.bcast)
                        add_low(st, i, par)
                        split(b + 5, 2 * par + 1)
                        if i == 0:
                            spread(st.bcast)
                        dve.wait_ge(lru_scaled, i + 1)
                        nc.vector.tensor_scalar(XC[:, i, :], xpad[:, i, CONV - 1:], cols[:, i, CONV - 1:CONV],
                                                cols[:, i, CONV_B:CONV_B + 1], ALU.mult, ALU.add).then_inc(tap_added, 1)
                        for n in range(1, CONV):
                            dve.wait_ge(tap_added, CONV * i + n)
                            tap = CONV - 1 - n
                            nc.vector.scalar_tensor_tensor(out=XC[:, i, :], in0=xpad[:, i, tap:tap + S],
                                                           scalar=cols[:, i, tap:tap + 1], in1=XC[:, i, :],
                                                           op0=ALU.mult, op1=ALU.add).then_inc(tap_added, 1)
                    if i >= 1:
                        dve.wait_ge(xc_hi, i)
                        nc.vector.tensor_tensor(H[:, i - 1, S:2 * S], XC[:, i - 1, :],
                                                H[:, i - 1, 0:S].bitcast(F32), ALU.subtract).then_inc(y_ready, 1)

            def gates(st):
                for i in range(KD):
                    if i % 2 == 0:
                        b = st.b0 + 4 + i // 2
                        split(b, b % RING)
                    reach(dve, gates_ready, i)
                    add_low(st, i, i % 2)
                for i in range(KD):
                    dve.wait_ge(decay_squared, i + 1)
                    nc.vector.scalar_tensor_tensor(out=TH[:, i, 1:], in0=RG[:, i, 1:], scalar=1.0, in1=TH[:, i, 1:],
                                                   op0=ALU.add, op1=ALU.mult)
                    nc.vector.memset(TH[:, i, 0:1], -1.0).then_inc(mult2_ready, 1)
                for i in range(KD):
                    dve.wait_ge(mult_ready, i + 1)
                    dve.wait_ge(gated, i + 1)
                    nc.vector.tensor_tensor(IG[:, i, :], RG[:, i, :], IG[:, i, :], ALU.mult).then_inc(input_ready, 1)
                    dve.wait_ge(input_ready, i + 1)
                    nc.vector.tensor_tensor_scan(TH[:, i, :], AA[:, i, :], IG[:, i, :], 0.0,
                                                 ALU.mult, ALU.add).then_inc(scanned, 1)
                    if i >= 1:
                        low_hy(i - 1)
                low_hy(KD - 1)

            def low_hy(i):
                dve.wait_ge(hy_hi, i + 1)
                nc.vector.tensor_tensor(H[:, i, S:2 * S], TH[:, i, :], H[:, i, 0:S].bitcast(F32),
                                        ALU.subtract).then_inc(y_ready, 1)

            for b in range(RING):
                split(b, b)
            dve.wait_ge(x_loaded, 32)
            dve.wait_ge(masks_set, MASKS)
            for d in range(KD):
                low_x(0, d)
            for st in stages:
                if st.kind == "up":
                    up(st)
                elif st.kind == "down":
                    down(st)
                elif st.kind == "out":
                    out_proj(st)
                elif st.kind == "nat":
                    nat(st)
                    if st.mixer == "moba":
                        turn_heads(st)
                        attend(st)
                        turn_out(st)
                elif st.kind == "lru_in":
                    lru_in(st)
                elif st.kind == "gates":
                    gates(st)
                elif st.kind == "compress":
                    windows()
                    turn_heads(st.nat_stage)
                    compress(st)
                    compressed_kv(st)
                    compressed_attention(st.nat_stage)
                    attend(st.nat_stage)
                    turn_out(st.nat_stage)

        @block.gpsimd
        def _(pool):
            def sum_squares(norm):
                for d in range(KD):
                    n = KD * norm + d
                    pool.wait_ge(squared, n + 1)
                    reach(pool, summed, n)
                    if d == 0:
                        nc.gpsimd.tensor_copy(ssum[:, :], sq[:, 0, :]).then_inc(summed, 1)
                    else:
                        nc.gpsimd.tensor_tensor(ssum[:, :], ssum[:, :], sq[:, d % 2, :], ALU.add).then_inc(summed, 1)

            def scale(st, i, first=False):
                pool.wait_ge(acc_free, st.o0 + 2 * i + 2)
                if first:
                    pool.wait_ge(rb_ready, st.bcast + 1)
                nc.gpsimd.tensor_tensor(gu[:, :, :], pre[:, :, :], rb[:, :].unsqueeze(1).to_broadcast([P, 2, S]),
                                        ALU.mult).then_inc(scaled, 1)

            def nsa_zero(st):
                pool.wait_ge(acc_free, st.o0 + 1)
                nc.gpsimd.memset(HV[:, :, :, :, :], 0.0).then_inc(nsa_zeroed, 1)
                nc.gpsimd.memset(PC[:, :, :, :], 0.0).then_inc(nsa_zeroed, 1)

            def compress(st):
                pool.wait_ge(nsa_zeroed, 2)
                pool.wait_ge(hidden_ready, 2)
                for hid in range(2):
                    src = hc[:, 1, hid, :].rearrange("p (g n) -> p g n", g=GROUPS).unsqueeze(2).to_broadcast(
                        [P, GROUPS, HPG, NCMP])
                    nc.gpsimd.tensor_copy(HV[:, hid, :, :, 0:NCMP], src).then_inc(hidden_spread, 1)

            def nat(st):
                if st.mixer == "nsa":
                    nsa_zero(st)
                ps = parts[st.mixer, st.j]
                n = 8 * st.nat
                for part in ps:
                    for tt in range(TT):
                        n += 1
                        pool.wait_ge(acc_free, st.o0 + 2 * part.chunk + 2)
                        reach(pool, heads_summed, n - 2)
                        x = QKV[:, tt, part.col:part.col + part.heads * HD]
                        nc.gpsimd.tensor_tensor(sqh[:, n % 2, 0:part.heads * HD], x, x, ALU.mult
                                                ).then_inc(heads_squared, 1)
                n = 8 * st.nat
                for part in ps:
                    for tt in range(TT):
                        n += 1
                        pool.wait_ge(heads_scaled, n)
                        x = QKV[:, tt, part.col:part.col + part.heads * HD].rearrange("p (a b) -> p a b", b=HD)
                        g = hgain[:, part.gain, :].unsqueeze(1).to_broadcast([P, part.heads, HD])
                        if part.col in (KS_COL, KW_COL) and st.mixer == "nsa":
                            dst = (KSD if part.col == KS_COL else KWD)[:, tt]
                            for e in range(2):
                                last = nc.gpsimd.tensor_tensor(dst[:, :, e, :], x, g, ALU.mult)
                            last.then_inc(heads_gained, 1)
                        else:
                            nc.gpsimd.tensor_tensor(x, x, g, ALU.mult).then_inc(heads_gained, 1)

            def lru_in(st):
                nc.gpsimd.memset(xpad[:, :, 0:CONV - 1], 0.0).then_inc(pad_set, 1)
                for i in range(KD):
                    pool.wait_ge(acc_free, st.o0 + 2 * i + 2)
                    if i == 0:
                        pool.wait_ge(rb_ready, st.bcast + 1)
                        pool.wait_ge(pad_set, 1)
                    reach(pool, gelu_done, i)
                    nc.gpsimd.tensor_tensor(xpad[:, i, CONV - 1:], pre[:, 0, :], rb[:, :], ALU.mult)
                    nc.gpsimd.tensor_tensor(gu[:, 1, :], pre[:, 1, :], rb[:, :], ALU.mult).then_inc(lru_scaled, 1)

            def gates(st):
                for i in range(KD):
                    pool.wait_ge(gates_ready, i + 1)
                    nc.gpsimd.tensor_tensor(IG[:, i, :], IG[:, i, :], XC[:, i, :], ALU.mult).then_inc(gated, 1)
                for i in range(KD):
                    pool.wait_ge(decay_ready, i + 1)
                    nc.gpsimd.tensor_tensor(RG[:, i, :], AA[:, i, :], AA[:, i, :], ALU.mult
                                            ).then_inc(decay_squared, 1)
                for i in range(KD):
                    pool.wait_ge(scanned, i + 1)
                    nc.gpsimd.tensor_tensor(TH[:, i, :], TH[:, i, :], YG[:, i, :], ALU.mult).then_inc(hy_ready, 1)

            for name, dst in const_loads:
                pool.dma_start(dst, t[name]).then_inc(consts_loaded, 16)
            nc.gpsimd.memset(eps[:, :], EPS).then_inc(eps_set, 1)
            nc.gpsimd.memset(ones[:, :], 1.0).then_inc(masks_set, 1)
            nc.gpsimd.memset(ident[:, :], 0.0).then_inc(masks_set, 1)
            nc.gpsimd.memset(tri[:, :, :], 0.0).then_inc(masks_set, 1)
            pool.wait_ge(masks_set, 3)
            nc.gpsimd.affine_select(out=ident[:, :], in_=ident[:, :], compare_op=ALU.not_equal, fill=1.0, base=0,
                                    pattern=[[-1, P]], channel_multiplier=1).then_inc(masks_set, 1)
            for a in (0, 2):
                nc.gpsimd.affine_select(out=tri[:, a, :], in_=tri[:, a, :], compare_op=ALU.is_ge, fill=NEG, base=0,
                                        pattern=[[-1, P]], channel_multiplier=1).then_inc(masks_set, 1)
            nc.gpsimd.memset(cmask[:, 0, :, :], 0.0).then_inc(masks_set, 1)
            nc.gpsimd.memset(cmask[:, 1, :, :], 1.0).then_inc(masks_set, 1)
            nc.gpsimd.memset(blk[:, :], 0.0).then_inc(masks_set, 1)
            pool.wait_ge(masks_set, 9)
            nc.gpsimd.memset(blk[0:HD, 0:HD], 1.0).then_inc(masks_set, 1)
            nc.gpsimd.memset(blk[HD:P, HD:P], 1.0).then_inc(masks_set, 1)
            pool.wait_ge(masks_set, 11)
            for m, fill in ((0, NEG), (1, 0.0)):
                nc.gpsimd.affine_select(out=cmask[:, m, :, :], in_=cmask[:, m, :, :], compare_op=ALU.is_ge, fill=fill,
                                        base=1 - CMP_L, pattern=[[P, TT], [-CMP_D, NCMP]],
                                        channel_multiplier=1).then_inc(masks_set, 1)
            sum_squares(0)
            pool.wait_ge(consts_loaded, 16 * CONSTS)
            for st in stages:
                if st.kind == "up":
                    scale(st, 0, first=True)
                    with nc.gpsimd.Fori(1, NF) as i:
                        scale(st, i)
                elif st.kind in ("down", "out"):
                    if st.upd + 1 < norms:
                        sum_squares(st.upd + 1)
                elif st.kind == "nat":
                    nat(st)
                elif st.kind == "lru_in":
                    lru_in(st)
                elif st.kind == "gates":
                    gates(st)
                elif st.kind == "compress":
                    compress(st)


MASKS = 13
LAM_STEPS = 15
CONV_B, BA, BX, LAM = range(CONV, CONV + 4)


def branch_of(mixer, n):
    if mixer == "moba":
        return n, 8 + n // 2, MOBA_V_COL + n * HD, None
    head, gate = n % HEADS, 1 + n // HEADS
    g = head // HPG
    return head, (8 if gate == 1 else 12) + g, (VS_COL if gate == 1 else VW_COL) + g * HD, gate


def stream_layout(w, cols):
    k, n = w.shape
    return w.reshape(k // P, P, n // cols, cols).transpose(2, 1, 0, 3).reshape(n // cols, P, k // P * cols)


def layout(depth, a):
    arrays = {}
    arrays["x"] = a["x"][0].T.reshape(KD, P, S).transpose(1, 0, 2)
    arrays["norm_g"] = a["norm_g"][0:depth].reshape(3 * depth, KD, P).transpose(2, 0, 1)
    ups, downs = [], []
    for layer in range(depth):
        for which in ("ffn1", "ffn2"):
            w = a[f"{which}_wi"][layer]
            blocks = stream_layout(w, P)
            ups.append(blocks.reshape(2, NF, P, BW).transpose(1, 0, 2, 3).reshape(2 * NF, P, BW))
            downs.append(stream_layout(a[f"{which}_wo"][layer], P))
    arrays["up_w"] = np.stack(ups)
    arrays["down_w"] = np.stack(downs)

    def token_major(w):
        n = w.shape[1]
        return w.reshape(4, 2, P, n).transpose(0, 2, 1, 3).reshape(4, P, 2 * n)

    arrays["moba_w"] = np.stack([np.concatenate([token_major(w[:, c:c + CHUNK]) for c in range(0, 3072, CHUNK)])
                                 for w in a["moba_w_in"]])
    arrays["moba_o"] = np.stack([stream_layout(w, P) for w in a["moba_w_out"]])
    arrays["hgain"] = np.concatenate([a["moba_q_gain"][0], a["moba_k_gain"][0], a["nsa_q_gain"][0],
                                      a["nsa_ks_gain"][0], a["nsa_kw_gain"][0], a["moba_q_gain"][1],
                                      a["moba_k_gain"][1]]).reshape(1, 7, HD).repeat(P, 0)
    arrays["lru_w"] = np.stack([stream_layout(w, P).reshape(2, KD, P, BW).transpose(1, 0, 2, 3).reshape(2 * KD, P, BW)
                                for w in a["lru_w_in"]])
    both = np.stack([a["lru_wa"], a["lru_wx"]], 2)[:, :, :].reshape(-1, 4, 2, 2, P, 2, P)
    arrays["lru_g"] = both.transpose(0, 1, 4, 5, 2, 3, 6).reshape(-1, 4, P, BW)
    arrays["lru_o"] = np.stack([stream_layout(w, P) for w in a["lru_w_out"]])
    w = a["nsa_w_in"]
    q, kc, vc, ks, vs, kw, vw, g = np.split(w, np.cumsum([D] + [GROUPS * HD] * 6), axis=-1)
    chunks = [np.concatenate([kc, vc], -1), q[:, :, 0:CHUNK], q[:, :, CHUNK:], np.concatenate([ks, vs], -1),
              np.concatenate([kw, vw], -1)]
    arrays["nsa_w"] = np.stack([np.concatenate([token_major(c[j]) for c in chunks]) for j in range(w.shape[0])])
    arrays["nsa_g"] = np.stack([token_major(x) for x in g])
    arrays["nsa_o"] = np.stack([stream_layout(w, P) for w in a["nsa_w_out"]])
    w1 = np.stack([a["nsa_ck_w1"], a["nsa_cv_w1"]], 1).reshape(-1, 2, 2, 8, P, 2, P)
    arrays["nsa_c"] = w1.transpose(0, 1, 5, 2, 4, 3, 6).reshape(-1, 8, P, BW)
    arrays["nsa_pos"] = np.stack([a["nsa_pos_k"][0], a["nsa_pos_v"][0]]).reshape(2, NPAIR, P).transpose(2, 0, 1)
    w2 = a["nsa_ck_w2"][0].reshape(2, P, HD).transpose(1, 0, 2)
    arrays["nsa_w2k"] = np.concatenate([w2, w2], -1)
    arrays["nsa_w2v"] = a["nsa_cv_w2"][0].reshape(2, P, HD).transpose(1, 0, 2)
    arrays["nsa_kc_gain"] = np.concatenate([a["nsa_kc_gain"][0]] * 2)[:, None]
    arrays["nsa_gate_b"] = a["nsa_gate_b"].repeat(P, 0)
    per_channel = [a["lru_conv_w"][0, n, 0] for n in range(CONV)] + [a[k][0] for k in
                                                                     ("lru_conv_b", "lru_ba", "lru_bx", "lru_lam")]
    arrays["lru_cols"] = np.stack(per_channel, -1).reshape(KD, P, CONV + 4).transpose(1, 0, 2)
    return {k: np.ascontiguousarray(v) for k, v in arrays.items()}


def kernel(**inputs):
    import concourse.bacc as bacc
    from concourse.bass_utils import run_bass_kernel_spmd

    arrays = layout(DEPTH, {k: np.asarray(v) for k, v in inputs.items()})
    nc = bacc.Bacc("TRN2", target_bir_lowering=False, num_devices=1)
    t = {k: nc.dram_tensor(f"in_{k}", v.shape, mybir.dt.from_np(v.dtype), kind="ExternalInput").ap()
         for k, v in arrays.items()}
    t["out"] = nc.dram_tensor("out", (P, KD, S), F32, kind="ExternalOutput").ap()
    trunk_program(nc, DEPTH, t)
    r = run_bass_kernel_spmd(nc, [{f"in_{k}": v for k, v in arrays.items()}], core_ids=[0])
    got = np.asarray(r.results[0]["out"])
    return np.ascontiguousarray(got.transpose(1, 0, 2).reshape(D, S).T[None])
```

```python
from contextlib import ExitStack

import numpy as np

import concourse.bass as bass
from concourse import mybir

F32 = mybir.dt.float32
F32R = mybir.dt.float32r
ALU = mybir.AluOpType
ACT = mybir.ActivationFunctionType
AX = mybir.AxisListType

P = 128
D = 1024
S = 256
DEPTH = 4
FF = 2816
EPS = 1e-6
NEG = -1e30
KD = D // P
NF = FF // P
TT = S // P
RING = 4
SLOTS = 8
BW = 8 * P
HEADS = 16
HD = 64
SCALE = HD ** -0.5
CHUNK = 512
CONV = 4
LRU_C = 8.0
GROUPS = 4
HPG = HEADS // GROUPS
CMP_L, CMP_D = 32, 16
NCMP = (S - CMP_L) // CMP_D + 1
CMP_HID = 256
NPAIR = CMP_L // 2
CN = GROUPS * NCMP
KINDS = ["moba", "lru", "nsa"]


class Stage:

    def __init__(self, kind, n_blocks, n_outs, **more):
        self.kind, self.n_blocks, self.n_outs = kind, n_blocks, n_outs
        self.b0 = self.o0 = 0
        self.w = more.get("w")
        self.mixer, self.j = more.get("mixer"), more.get("j")
        self.norm = more.get("norm")
        self.upd = more.get("upd")
        self.ffn, self.bcast, self.pair = more.get("ffn"), more.get("bcast"), more.get("pair")
        self.y, self.nat, self.branch = more.get("y"), more.get("nat"), more.get("branch")
        self.branches = more.get("branches")
        self.nat_stage = more.get("nat_stage")


def plan(depth):
    stages = []
    ffn = upd = bcast = y = nat = pair = branch = 0

    def add_ffn(layer, which):
        nonlocal ffn, upd, bcast, pair
        norm = 3 * layer + (0 if which == 0 else 2)
        stages.append(Stage("up", 2 * NF, 2 * NF, w=2 * layer + which, ffn=ffn, norm=norm, bcast=bcast, pair=pair))
        pair += NF
        stages.append(Stage("down", 3 * KD, KD, w=2 * layer + which, ffn=ffn, upd=upd,
                            mixer=KINDS[layer % 3] if which == 0 else None))
        ffn, upd, bcast = ffn + 1, upd + 1, bcast + 1

    for layer in range(depth):
        add_ffn(layer, 0)
        kind, j = KINDS[layer % 3], layer // 3
        norm = 3 * layer + 1
        if kind == "moba":
            stages.append(Stage("nat", 24, 12, mixer="moba", j=j, norm=norm, nat=nat, branch=branch, y=y,
                                branches=HEADS))
            nat, branch = nat + 1, branch + HEADS
        elif kind == "nsa":
            stages.append(Stage("nat", 24, 12, mixer="nsa", j=j, norm=norm, nat=nat, branch=branch, y=y,
                                branches=2 * HEADS))
            nat, branch = nat + 1, branch + 2 * HEADS
            stages.append(Stage("compress", 8, 0, mixer="nsa", j=j, nat_stage=stages[-1]))
        else:
            stages.append(Stage("lru_in", 16, 16, mixer="lru", j=j, norm=norm, bcast=bcast, y=y, pair=pair))
            bcast, y, pair = bcast + 1, y + 8, pair + 8
            stages.append(Stage("gates", 4, 0, mixer="lru", j=j, y=y))
        stages.append(Stage("out", 8, 8, mixer=kind, j=j, upd=upd, y=y))
        y += 8
        upd += 1
        add_ffn(layer, 1)
    b = o = 0
    for st in stages:
        st.b0, st.o0 = b, o
        b, o = b + st.n_blocks, o + st.n_outs
        assert b % RING == 0 and o % 4 == 0
    return stages, b


class Part:

    def __init__(self, chunk, col, heads, slot, gain):
        self.chunk, self.col, self.heads, self.slot, self.gain = chunk, col, heads, slot, gain


GAIN0 = {("moba", 0): 0, ("nsa", 0): 2, ("moba", 1): 5}
Q_COL = {"moba": 0, "nsa": 512}
KS_COL, VS_COL, KW_COL, VW_COL, G_COL = 1536, 1792, 2048, 2304, 2560
NG = 3 * HEADS
MOBA_V_COL = 2048


def parts_of(mixer, j):
    g = GAIN0[mixer, j]
    if mixer == "moba":
        return [Part(0, 0, 8, 0, g), Part(1, 512, 8, 8, g), Part(2, 1024, 8, 16, g + 1), Part(3, 1536, 8, 24, g + 1)]
    return [Part(1, 512, 8, 0, g), Part(2, 1024, 8, 8, g), Part(3, KS_COL, 4, 16, g + 1), Part(4, KW_COL, 4, 20, g + 2)]


def trunk_program(nc, depth, t):
    stages, n_blocks = plan(depth)
    norms = 3 * depth
    parts = {(st.mixer, st.j): parts_of(st.mixer, st.j) for st in stages if st.kind == "nat"}
    with ExitStack() as ctx:
        def sb(name, shape, dt=F32):
            return ctx.enter_context(nc.sbuf_tensor(name, shape, dt))

        def sem(name):
            return ctx.enter_context(nc.semaphore(name))

        def reach(eng, s, value):
            if not isinstance(value, int) or value > 0:
                eng.wait_ge(s, value)

        raw = sb("raw", [P, RING, BW])
        w_hi = sb("w_hi", [P, RING, BW], F32R)
        w_lo = sb("w_lo", [P, RING, BW], F32R)
        X = sb("X", [P, KD, 2 * S], F32R)
        H = sb("H", [P, NF, 2 * S], F32R)
        h = sb("h", [P, KD, S])
        gains = sb("gains", [P, norms, KD])
        sq = sb("sq", [P, 2, S])
        ssum = sb("ssum", [P, S])
        sd = sb("sd", [P, TT])
        rstd = sb("rstd", [P, TT])
        rdiag = sb("rdiag", [P, TT, P])
        rb = sb("rb", [P, S])
        eps = sb("eps", [P, 1])
        ones = sb("ones", [P, P])
        ident = sb("ident", [P, P])
        tri = sb("tri", [P, 3, P])
        pairbuf = sb("pairbuf", [P, 2, 2, S])
        bt = pairbuf[:, 0]
        pre = pairbuf[:, 1]
        sqh = pairbuf[:, :, :, :].rearrange("p a b c -> p a (b c)")
        gu = sb("gu", [P, 2, S])
        sg = sb("sg", [P, S])
        hf = sb("hf", [P, S])

        scratch = sb("scratch", [P, 12288])
        QKV = scratch[:, 0:6144].rearrange("p (t c) -> p t c", t=TT)
        QT = scratch[:, 6144:8192].rearrange("p (q s) -> p q s", s=S)
        KE = scratch[:, 8192:10240].rearrange("p (q s) -> p q s", s=S)
        O = scratch[:, 10240:12288].rearrange("p (t c) -> p t c", t=TT)
        ssh = sb("ssh", [P, TT, 32])
        sdh = sb("sdh", [P, TT, 32])
        rqh = sb("rqh", [P, TT, 32])
        hgain = sb("hgain", [P, 7, HD])
        rings = sb("rings", [P, 6 * 3 * P])
        SM, PR, PT = (rings[:, n * 768:(n + 1) * 768].rearrange("p (a b) -> p a b", a=2)
                      for n in range(3))
        mx = sb("mx", [P, SLOTS, TT])
        nm = sb("nm", [P, SLOTS, TT])
        sums = sb("sums", [P, SLOTS, TT])
        rsum = sb("rsum", [P, SLOTS, TT])
        cf = sb("cf", [P, SLOTS, TT])

        xpad_all = sb("xpad", [P, KD * (S + CONV - 1)])
        xpad = xpad_all[:, :].rearrange("p (k s) -> p k s", s=S + CONV - 1)
        XC, YG, RG, IG, AA, TH = (scratch[:, n * 2048:(n + 1) * 2048].rearrange("p (k s) -> p k s", s=S)
                                  for n in range(6))
        cols = sb("cols", [P, KD, CONV + 4])
        lam = sb("lam", [P, 8, KD])
        loga = sb("loga", [P, KD])

        gbias = sb("gbias", [P, NG])
        G = sb("G", [P, TT, NG])
        pos = sb("pos", [P, 2, NPAIR])
        w2k = sb("w2k", [P, 2, P])
        w2v = sb("w2v", [P, 2, HD])
        kcgain = sb("kcgain", [P, 1])
        x2f = scratch[:, 10240:10240 + 2 * NPAIR * CN].rearrange("p (a m n) -> p a m n", a=2, n=CN)
        X2 = H[:, 8:16, :].rearrange("p f s -> p (f s)")[:, 0:4 * NPAIR * CN].rearrange(
            "p (a m n) -> p a m n", a=2, n=2 * CN)
        KO_T = {"moba": xpad_all[:, 0:2048].rearrange("p (t q s) -> p t q s", t=2, s=S),
                "nsa": QKV[:, :, Q_COL["nsa"]:KS_COL].rearrange("p t (q s) -> p t q s", s=S)}
        hct = pairbuf[:, 0]
        hc = sb("hc", [P, 2, 2, CN])
        HV = QKV[:, :, G_COL:3072].rearrange("p k (g r n) -> p k g r n", g=GROUPS, r=HPG)
        blk = sb("blk", [P, P])
        sqc = sb("sqc", [P, 3, CN])
        KCP = sb("KCP", [P, GROUPS, 2, 16])
        VC = sb("VC", [P, GROUPS, HD])
        VCB = QKV[:, :, 0:512].rearrange("p t (g r d) -> p t g r d", r=HPG, d=HD)
        cmask = sb("cmask", [P, 2, TT, NCMP])
        SC, PCE = (QKV[:, i, 0:512].rearrange("p (t h n) -> p t h n", t=TT, h=HEADS) for i in range(2))
        cst = sb("cst", [P, 4, TT * HEADS])
        PC = xpad_all[:, 0:1024].rearrange("p (t h n) -> p t h n", t=TT, h=HEADS)
        KVD = O.rearrange("p t (g e d) -> p t g e d", e=2, d=HD)
        KSD = rings[:, 1024:2048].rearrange("p (t g e d) -> p t g e d", t=TT, e=2, d=HD)
        KWD = xpad_all[:, 1024:2048].rearrange("p (t g e d) -> p t g e d", t=TT, e=2, d=HD)
        PCT = xpad_all[:, 1024:2048].rearrange("p (t c) -> p t c", t=TT)

        PS = ctx.enter_context(nc.psum_tensor("PS", [P, 8, 512], F32))
        STAT = 6

        block_loaded = [sem(f"block_loaded{i}") for i in range(RING)]
        hi_ready, lo_ready, blocks_used = sem("hi_ready"), sem("lo_ready"), sem("blocks_used")
        acc_free, low_copied = sem("acc_free"), sem("low_copied")
        x_loaded = [sem("x_loaded0"), sem("x_loaded1")]
        consts_loaded, out_stored = sem("consts_loaded"), sem("out_stored")
        masks_set, eps_set = sem("masks_set"), sem("eps_set")
        xhi_ready, x_ready = sem("xhi_ready"), sem("x_ready")
        squared, summed = sem("squared"), sem("summed")
        stat_full, sd_ready, rstd_ready = sem("stat_full"), sem("sd_ready"), sem("rstd_ready")
        diag_ready, rb_full, rb_ready = sem("diag_ready"), sem("rb_full"), sem("rb_ready")
        half_added = sem("half_added")
        scaled, silu_ready, prod_ready = sem("scaled"), sem("silu_ready"), sem("prod_ready")
        hhi_ready, h_ready = sem("hhi_ready"), sem("h_ready")
        heads_squared, heads_summed, head_sd, head_rms = (sem("heads_squared"), sem("heads_summed"),
                                                          sem("head_sd"), sem("head_rms"))
        heads_scaled, heads_gained, keys_zeroed = sem("heads_scaled"), sem("heads_gained"), sem("keys_zeroed")
        turned, turned_act, turned_dve = sem("turned"), sem("turned_act"), sem("turned_dve")
        scores_full, masked, negmax, probs_ready = sem("scores_full"), sem("masked"), sem("negmax"), sem("probs_ready")
        pt_full, pt_ready, o_full, o_done = sem("pt_full"), sem("pt_ready"), sem("o_full"), sem("o_done")
        sum_inv, coef_ready = sem("sum_inv"), sem("coef_ready")
        ot_full, yhi_ready, y_ready = sem("ot_full"), sem("yhi_ready"), sem("y_ready")
        pad_set, lru_scaled, gelu_done = sem("pad_set"), sem("lru_scaled"), sem("gelu_done")
        tap_added, xc_hi, gates_ready = sem("tap_added"), sem("xc_hi"), sem("gates_ready")
        gate_sums, log_ready = sem("gate_sums"), sem("log_ready")
        lam_exp, lam_step = sem("lam_exp"), sem("lam_step")
        decay_ready, decay_squared, gated = sem("decay_ready"), sem("decay_squared"), sem("gated")
        mult2_ready, mult_ready, input_ready = sem("mult2_ready"), sem("mult_ready"), sem("input_ready")
        scanned, hy_ready, hy_hi = sem("scanned"), sem("hy_ready"), sem("hy_hi")
        win_turned, win_ready, win_hi, win_low = sem("win_turned"), sem("win_ready"), sem("win_hi"), sem("win_low")
        gate_ready = sem("gate_ready")
        nsa_zeroed, hidden_ready, hidden_spread = sem("nsa_zeroed"), sem("hidden_ready"), sem("hidden_spread")
        hidden_turned, hidden_copied = sem("hidden_turned"), sem("hidden_copied")
        kc_full, kc_squared, kc_summed, kc_sd = sem("kc_full"), sem("kc_squared"), sem("kc_summed"), sem("kc_sd")
        kc_inv, kc_ready, vc_full, vc_ready = sem("kc_inv"), sem("kc_ready"), sem("vc_full"), sem("vc_ready")
        sc_full, sc_step, pce_ready = sem("sc_full"), sem("sc_step"), sem("pce_ready")
        pc_ready, pct_full, pct_ready = sem("pc_ready"), sem("pct_full"), sem("pct_ready")
        values_spread = sem("values_spread")
        oc_full, oc_done = sem("oc_full"), sem("oc_done")

        const_loads = [("hgain", hgain[:, :, :]), ("lru_cols", cols[:, :, :]), ("nsa_gate_b", gbias[:, :]),
                       ("nsa_pos", pos[:, :, :]), ("nsa_w2k", w2k[:, :, :]), ("nsa_w2v", w2v[:, :, :]),
                       ("nsa_kc_gain", kcgain[:, :])]
        CONSTS = len(const_loads)

        def turned_tiles(mixer, q):
            src = PS[:, 4 + q % 4, :].rearrange("p (a s) -> p a s", a=2)
            if q < 4:
                return [(QT[:, 2 * q:2 * q + 2, :], src)]
            kt = 2 * q - 8
            return [(KE[0:HD, kt:kt + 2, :], src[0:HD]),
                    (KO_T[mixer][HD:P, kt // 4, kt % 4:kt % 4 + 2, :], src[HD:P])]

        block = ctx.enter_context(nc.Block())

        def conv_cols(b):
            for st in stages:
                if st.b0 <= b < st.b0 + st.n_blocks:
                    i = b - st.b0
                    if st.kind == "down" and i % 3 == 2:
                        return (NF - 16) * P
                    if st.kind == "nat" and st.mixer == "nsa" and i >= 20:
                        return 2 * NG
                    return BW

        @block.sync
        def _(sp):
            def load(b, ring, src, n=BW):
                reach(sp, lo_ready, b - RING + 1)
                sp.dma_start(raw[:, ring, 0:n], src).then_inc(block_loaded[ring], 16)

            def down_src(w, d, s):
                n = BW if s < 2 else (NF - 16) * P
                return t["down_w"][w, d][:, s * BW:s * BW + n], n

            sp.dma_start(gains[:, :, :], t["norm_g"]).then_inc(x_loaded[0], 16)
            for half in range(2):
                cut = slice(half * KD // 2, (half + 1) * KD // 2)
                sp.dma_start(h[:, cut, :], t["x"][:, cut, :]).then_inc(x_loaded[half], 16)
            for st in stages:
                b0 = st.b0
                if st.kind == "up":
                    first = 0
                    if b0 == 0:
                        first = 1
                        for s in range(4):
                            load(s, s, t["up_w"][st.w, s])
                    with sp.Fori(first, 2 * NF // 4) as it:
                        for s in range(4):
                            load(b0 + 4 * it + s, s, t["up_w"][st.w, 4 * it + s])
                elif st.kind == "down":
                    with sp.Fori(0, KD // 4) as it:
                        for d in range(4):
                            for s in range(3):
                                src, n = down_src(st.w, 4 * it + d, s)
                                load(b0 + 12 * it + 3 * d + s, (3 * d + s) % RING, src, n)
                elif st.kind == "nat" and st.mixer == "nsa":
                    with sp.Fori(0, 5) as it:
                        for s in range(4):
                            load(b0 + 4 * it + s, s, t["nsa_w"][st.j, 4 * it + s])
                    for s in range(4):
                        load(b0 + 20 + s, s, t["nsa_g"][st.j, s], 2 * NG)
                else:
                    arr = {"nat": "moba_w", "lru_in": "lru_w", "gates": "lru_g", "compress": "nsa_c",
                           "out": st.mixer + "_o"}[st.kind]
                    with sp.Fori(0, st.n_blocks // 4) as it:
                        for s in range(4):
                            load(b0 + 4 * it + s, s, t[arr][st.j, 4 * it + s])
            last = stages[-1]
            for d in range(KD):
                sp.wait_ge(acc_free, last.o0 + d + 1)
                sp.dma_start(t["out"][:, d, :], h[:, d, :]).then_inc(out_stored, 16)
            sp.wait_ge(out_stored, 16 * KD)

        @block.tensor
        def _(pe):
            mm = nc.tensor.matmul

            def tile(bank, ring, col, rhs, n, first, last):
                mm(PS[:, bank, 0:2 * n], w_hi[:, ring, col:col + P], rhs[:, 0:2 * n], start=first, stop=False,
                   skip_group_check=True)
                return mm(PS[:, bank, 0:n], w_lo[:, ring, col:col + P], rhs[:, 0:n], start=False, stop=last,
                          skip_group_check=True)

            def stats(norm):
                pe.wait_ge(summed, KD * (norm + 1))
                for tt in range(TT):
                    last = mm(PS[:, STAT, tt:tt + 1], ssum[:, tt * P:(tt + 1) * P], ones[:, 0:1], start=True, stop=True)
                last.then_inc(stat_full, 1)

            def spread(nb):
                pe.wait_ge(diag_ready, nb + 1)
                mm(PS[:, STAT, 256:512], ones[:, :], rdiag[:, :, :], start=True, stop=True).then_inc(rb_full, 1)

            def pair(st, i, par, peeled=False):
                for g in range(2):
                    b, ring = st.b0 + 2 * i + g, (2 * par + g) % RING
                    pe.wait_ge(lo_ready, b + 1)
                    reach(pe, acc_free, st.o0 + 2 * i + g - 3)
                    for k in range(KD):
                        if peeled and i == 0 and g == 0:
                            pe.wait_ge(x_ready, KD * st.norm + k + 1)
                        last = tile(2 * par + g, ring, k * P, X[:, k, :], S, k == 0, k == KD - 1)
                    last.then_inc(blocks_used, 1)
                    if peeled and (i, g) == (0, 1):
                        stats(st.norm)
                    if peeled and (i, g) == (1, 0):
                        spread(st.bcast)

            def up(st):
                n = st.n_outs // 2
                for i in range(2):
                    pair(st, i, i, peeled=True)
                with nc.tensor.Fori(1, n // 2) as it:
                    for s in range(2):
                        pair(st, 2 * it + s, s)

            def down(st):
                with nc.tensor.Fori(0, KD // 4) as it:
                    for d in range(4):
                        reach(pe, acc_free, st.o0 + 4 * it + d - 3)
                        for s in range(3):
                            b, ring = st.b0 + 12 * it + 3 * d + s, (3 * d + s) % RING
                            pe.wait_ge(lo_ready, b + 1)
                            hi = min(8 * s + 8, NF)
                            pe.wait_ge(h_ready, NF * st.ffn + hi)
                            for f in range(8 * s, hi):
                                last = tile(d, ring, (f - 8 * s) * P, H[:, f, :], S, f == 0, f == NF - 1)
                            last.then_inc(blocks_used, 1)

            def out_proj(st):
                first = 0
                if st.mixer == "lru":
                    first = 1
                    pe.wait_ge(gates_ready, KD)
                    pe.wait_ge(lo_ready, st.b0 + 4)
                    for k in range(KD):
                        pe.wait_ge(y_ready, st.y + k + 1)
                        for d in range(4):
                            last = tile(d, d, k * P, H[:, k, :], S, k == 0, k == KD - 1)
                            if k == KD - 1:
                                last.then_inc(blocks_used, 1)
                with nc.tensor.Fori(first, KD // 4) as it:
                    for d in range(4):
                        reach(pe, acc_free, st.o0 + 4 * it + d - 3)
                        pe.wait_ge(lo_ready, st.b0 + 4 * it + d + 1)
                        for k in range(KD):
                            if d == 0 and k % 2 == 0:
                                pe.wait_ge(y_ready, st.y + k + 2)
                            last = tile(d, d, k * P, H[:, k, :], S, k == 0, k == KD - 1)
                        last.then_inc(blocks_used, 1)

            def chunk(st, c, par, n=CHUNK):
                for q in range(4):
                    quarter(st, c, par, q, n)

            def quarter(st, c, par, q, n=CHUNK, first=False):
                if q == 0:
                    pe.wait_ge(acc_free, st.o0 + 2 * c - 2)
                pe.wait_ge(lo_ready, st.b0 + 4 * c + q + 1)
                for kk in range(2):
                    k = 2 * q + kk
                    if first:
                        pe.wait_ge(x_ready, KD * st.norm + k + 1)
                    for tt in range(TT):
                        out = PS[:, 2 * par + tt, 0:n]
                        x_hi, x_lo = (X[:, k, o + tt * P:o + (tt + 1) * P] for o in (0, S))
                        hi, lo = (w[:, q, kk * n:(kk + 1) * n] for w in (w_hi, w_lo))
                        mm(out, x_hi, hi, start=(k == 0), stop=False)
                        mm(out, x_hi, lo, start=False, stop=False)
                        last = mm(out, x_lo, hi, start=False, stop=(k == KD - 1))
                last.then_inc(blocks_used, 1)

            def nat(st):
                for q in range(4):
                    quarter(st, 0, 0, q, first=True)
                    if q == 1:
                        stats(st.norm)
                for c in range(1, 4):
                    chunk(st, c, c % 2)
                if st.mixer == "nsa":
                    turn_windows(st)
                    chunk(st, 4, 0)
                    pe.wait_ge(win_ready, 8)
                    turn_heads(st, range(0, 4))
                    chunk(st, 5, 1, NG)
                else:
                    turn_heads(st, range(0, 4))
                    chunk(st, 4, 0)

            def turn_heads(st, banks):
                for q in banks:
                    n = 8 * st.nat + q
                    pe.wait_ge(heads_gained, 8 * st.nat + (4 if q < 4 else 8))
                    if q >= 4:
                        pe.wait_ge((turned_act, turned_dve)[q % 2], TURNED * st.nat + (q - 4) // 2 + 1)
                    for i in range(2):
                        tl = 2 * q + i
                        for tt in range(TT):
                            if st.mixer == "moba":
                                src = QKV[:, tt, tl * P:(tl + 1) * P]
                            elif tl < 8:
                                c = Q_COL["nsa"] + tl * P
                                src = QKV[:, tt, c:c + P]
                            else:
                                src = (KSD, KWD)[(tl - 8) // 4][:, tt, tl % 4, :, :].rearrange("p e d -> p (e d)")
                            last = nc.tensor.transpose(PS[:, 4 + q % 4, i * S + tt * P:i * S + (tt + 1) * P],
                                                       src, ident[:, :])
                    last.then_inc(turned, 1)

            def attend(st):
                pe.wait_ge(acc_free, st.o0 + (10 if st.mixer == "moba" else 12))
                if st.mixer == "nsa":
                    pe.wait_ge(hidden_ready, 2)
                for n in range(st.branches + 3):
                    if st.mixer == "nsa":
                        compressed_step(n)
                    elif 1 <= n <= 4:
                        quarter(st, 5, 1, n - 1)
                    if n < st.branches:
                        head, kt, _, _ = branch_of(st.mixer, n)
                        a = st.branch + n
                        if n == 0:
                            pe.wait_ge(turned_act, TURNED * st.nat + 4)
                        elif n == 1:
                            pe.wait_ge(turned_dve, TURNED * st.nat + 4)
                        elif n == 2:
                            pe.wait_ge(turned_act, TURNED * (st.nat + 1))
                            pe.wait_ge(turned_dve, TURNED * (st.nat + 1))
                        keys = KE[:, kt, :] if head % 2 == 0 else KO_T[st.mixer][:, kt // 4, kt % 4, :]
                        reach(pe, masked, a - 1)
                        mm(PS[:, 4 + n % 2, 0:P], QT[:, head // 2, 0:P], keys[:, 0:P], start=True, stop=True)
                        mm(PS[:, 4 + n % 2, P:3 * P], QT[:, head // 2, P:2 * P], keys,
                           start=True, stop=True).then_inc(scores_full, 1)
                    if 2 <= n < st.branches + 2:
                        m, a = n - 2, st.branch + n - 2
                        pe.wait_ge(probs_ready, a + 1)
                        reach(pe, pt_ready, a - 1)
                        for i in range(3):
                            last = nc.tensor.transpose(PS[:, 6 + m % 2, i * P:(i + 1) * P],
                                                       PR[:, m % 2, i * P:(i + 1) * P], ident[:, :])
                        last.then_inc(pt_full, 1)
                    if n >= 3:
                        m = n - 3
                        _, _, v, _ = branch_of(st.mixer, m)
                        a = st.branch + m
                        if st.mixer == "moba" and m == 8:
                            pe.wait_ge(acc_free, st.o0 + 12)
                        pe.wait_ge(pt_ready, a + 1)
                        reach(pe, o_done, a - 1)
                        pt = PT[:, m % 2, :]
                        mm(PS[:, m % 2, 0:HD], pt[:, 0:P], QKV[:, 0, v:v + HD], start=True, stop=True)
                        mm(PS[:, m % 2, HD:2 * HD], pt[:, P:2 * P], QKV[:, 0, v:v + HD], start=True, stop=False)
                        mm(PS[:, m % 2, HD:2 * HD], pt[:, 2 * P:3 * P], QKV[:, 1, v:v + HD], start=False,
                           stop=True).then_inc(o_full, 1)

            def turn_out(st):
                pe.wait_ge(o_done, st.branch + st.branches)
                for q in range(4):
                    for i in range(2):
                        for tt in range(TT):
                            last = nc.tensor.transpose(PS[:, 4 + q, i * S + tt * P:i * S + (tt + 1) * P],
                                                       O[:, tt, (2 * q + i) * P:(2 * q + i + 1) * P], ident[:, :])
                    last.then_inc(ot_full, 1)

            def turn_windows(st):
                pe.wait_ge(acc_free, st.o0 + 2)
                for kv in range(2):
                    for g in range(GROUPS):
                        for tt in range(TT):
                            c = (g % 2) * S + tt * P
                            last = nc.tensor.transpose(PS[:, 4 + 2 * kv + g // 2, c:c + P],
                                                       KVD[:, tt, kv * GROUPS + g, :, :].rearrange("p e d -> p (e d)"),
                                                       ident[:, :])
                    last.then_inc(win_turned, 1)

            def compress(st):
                for kv in range(2):
                    pe.wait_ge(win_low, kv + 1)
                    if kv == 0:
                        pe.wait_ge(acc_free, st.o0 - 2)
                    for q in range(4):
                        b = 4 * kv + q
                        pe.wait_ge(lo_ready, st.b0 + b + 1)
                        for i in range(4):
                            m = 4 * q + i
                            x_hi, x_lo = (X2[:, kv, m, o:o + CN] for o in (0, CN))
                            hi, lo = (w[:, q, i * CMP_HID:(i + 1) * CMP_HID] for w in (w_hi, w_lo))
                            out = PS[0:CN, kv, 0:CMP_HID]
                            mm(out, x_hi, hi, start=(m == 0), stop=False)
                            mm(out, x_hi, lo, start=False, stop=False)
                            last = mm(out, x_lo, hi, start=False, stop=(m == NPAIR - 1))
                        last.then_inc(blocks_used, 1)
                        if b == 5:
                            turn_hidden(0)
                        elif b == 6:
                            compressed_keys()
                        elif b == 7:
                            pe.wait_ge(kc_squared, 1)
                            mm(PS[:, 5, 0:CN], blk[:, :], sqc[:, 0, :], start=True, stop=True).then_inc(kc_summed, 1)
                turn_hidden(1)

            def turn_hidden(kv):
                pe.wait_ge(hidden_ready, kv + 1)
                if kv == 0:
                    pe.wait_ge(turned_act, TURNED * nsa_nat + 2)
                    pe.wait_ge(turned_dve, TURNED * nsa_nat + 2)
                for hid in range(2):
                    last = nc.tensor.transpose(PS[:, 6 + kv, hid * CN:(hid + 1) * CN],
                                               hct[0:CN, kv, hid * P:(hid + 1) * P], ident[0:CN, 0:CN])
                last.then_inc(hidden_turned, 1)

            def compressed_keys():
                pe.wait_ge(hidden_copied, 1)
                for hid in range(2):
                    last = mm(PS[:, 4, 0:CN], w2k[:, hid, :], hc[:, 0, hid, :], start=(hid == 0), stop=(hid == 1))
                last.then_inc(kc_full, 1)

            def compressed_step(n):
                if n in CMP_SCORES:
                    q = n - CMP_SCORES[0]
                    tt = q // 2
                    for pr in range(4 * (q % 2), 4 * (q % 2) + 4):
                        last = mm(PS[:, 2, (tt * 8 + pr) * 32:(tt * 8 + pr + 1) * 32],
                                  QT[:, pr, tt * P:(tt + 1) * P], KCP[:, 2 * pr // HPG, :, :], start=True, stop=True)
                    last.then_inc(sc_full, 1)
                elif n in CMP_VALUES:
                    q = n - CMP_VALUES[0]
                    pe.wait_ge(hidden_spread, 2)
                    for g in (2 * q, 2 * q + 1):
                        for hid in range(2):
                            last = mm(PS[:, 3, 256 + g * HD:256 + (g + 1) * HD], HV[:, hid, g, :, :], w2v[:, hid, :],
                                      start=(hid == 0), stop=(hid == 1))
                    last.then_inc(vc_full, 1)
                elif n == CMP_TURN:
                    pe.wait_ge(vc_ready, 1)
                    pe.wait_ge(pc_ready, 1)
                    for tt in range(TT):
                        for g in range(GROUPS):
                            last = nc.tensor.transpose(PS[:, 2 + tt, g * P:(g + 1) * P],
                                                       PC[:, tt, HPG * g:HPG * (g + 1), :], ident[:, :])
                        last.then_inc(pct_full, 1)
                elif n in CMP_OUT:
                    tt, half = divmod(CMP_OUT.index(n), 2)
                    pe.wait_ge(pct_ready, 2)
                    pe.wait_ge(values_spread, 1 + HPG)
                    reach(pe, oc_done, 2 * tt)
                    for g in range(2):
                        last = mm(PS[:, 2 + half, g * S:(g + 1) * S],
                                  PCT[:, tt, (2 * half + g) * P:(2 * half + g + 1) * P], VCB[:, half, g, :, :],
                                  start=True, stop=True)
                    last.then_inc(oc_full, 1)

            def gates(st):
                for q in range(4):
                    pe.wait_ge(lo_ready, st.b0 + q + 1)
                    pe.wait_ge(y_ready, st.y - 8 + 2 * q + 2)
                    for i in range(2):
                        out = 2 * q + i
                        if out < 4:
                            pe.wait_ge(acc_free, st.o0 - (2 if out == 0 else 0))
                        else:
                            pe.wait_ge(gates_ready, out - 3)
                        for g in range(2):
                            acc = PS[:, 2 * (out % 4) + g, 0:S]
                            for kt in range(2):
                                c = (4 * i + 2 * g + kt) * P
                                x_hi, x_lo = (H[:, 2 * q + kt, o:o + S] for o in (0, S))
                                hi, lo = (w[:, q, c:c + P] for w in (w_hi, w_lo))
                                mm(acc, hi, x_hi, start=(kt == 0), stop=False)
                                mm(acc, hi, x_lo, start=False, stop=False)
                                last = mm(acc, lo, x_hi, start=False, stop=(kt == 1))
                        if i == 0:
                            last.then_inc(gate_sums, 1)
                    last.then_inc(blocks_used, 1)

            pe.wait_ge(masks_set, MASKS)
            nsa_nat = sum(st.nat for st in stages if st.kind == "nat" and st.mixer == "nsa")
            for st in stages:
                if st.kind in ("up", "lru_in"):
                    up(st)
                elif st.kind == "down":
                    down(st)
                elif st.kind == "out":
                    out_proj(st)
                elif st.kind == "nat":
                    nat(st)
                    if st.mixer == "moba":
                        turn_heads(st, range(4, 8))
                        attend(st)
                        turn_out(st)
                elif st.kind == "gates":
                    gates(st)
                elif st.kind == "compress":
                    compress(st)
                    pe.wait_ge(kc_ready, 2)
                    pe.wait_ge(hidden_copied, 2)
                    turn_heads(st.nat_stage, range(4, 8))
                    attend(st.nat_stage)
                    turn_out(st.nat_stage)

        @block.scalar
        def _(act):
            def split(b, ring, n=None, loaded=None):
                if isinstance(b, int):
                    if b >= n_blocks:
                        return
                    n, loaded = conv_cols(b), b // RING + 1
                act.wait_ge(block_loaded[ring], 16 * loaded)
                reach(act, blocks_used, b - RING + 1)
                nc.scalar.copy(w_hi[:, ring, 0:n], raw[:, ring, 0:n]).then_inc(hi_ready, 1)

            def square_and_round(norm, d):
                if norm * KD + d >= 2:
                    act.wait_ge(summed, norm * KD + d - 1)
                nc.scalar.activation(sq[:, d % 2, :], h[:, d, :], ACT.Square).then_inc(squared, 1)
                nc.scalar.activation(X[:, d, 0:S], h[:, d, :], ACT.Copy,
                                     scale=gains[:, norm, d:d + 1]).then_inc(xhi_ready, 1)

            def stats(norm):
                act.wait_ge(stat_full, norm + 1)
                nc.scalar.activation(sd[:, :], PS[:, STAT, 0:TT], ACT.Sqrt, scale=1.0 / D,
                                     bias=eps[:, 0:1]).then_inc(sd_ready, 1)

            def copy_low(st, i, par, used):
                act.wait_ge(blocks_used, used)
                nc.scalar.copy(bt[:, :, :], PS[:, 2 * par:2 * par + 2, S:2 * S]).then_inc(low_copied, 1)

            def round_hidden(st, i):
                act.wait_ge(prod_ready, NF * st.ffn + i + 1)
                nc.scalar.copy(H[:, i, 0:S], hf[:, :]).then_inc(hhi_ready, 1)

            def up_step(st, i, par, it=None, first=False):
                b = st.b0 + 2 * i
                dyn = dict(n=BW, loaded=it) if it is not None else {}
                split(b + 4, 2 * par, **dyn)
                if first:
                    stats(st.norm)
                copy_low(st, i, par, b + 2)
                if not first:
                    round_hidden(st, i - 1)
                split(b + 5, 2 * par + 1, **dyn)
                act.wait_ge(scaled, NF * st.ffn + i + 1)
                nc.scalar.activation(sg[:, :], gu[:, 0, :], ACT.Silu).then_inc(silu_ready, 1)

            def up(st):
                up_step(st, 0, 0, first=True)
                up_step(st, 1, 1)
                with nc.scalar.Fori(1, NF // 2 - 1) as it:
                    for s in range(2):
                        up_step(st, 2 * it + s, s, it=st.b0 // RING + it + 2)
                for i in (NF - 2, NF - 1):
                    up_step(st, i, i % 2)
                round_hidden(st, NF - 1)

            def down(st):
                for d in range(KD):
                    if st.mixer == "lru" and d == 1:
                        lambda_exp()
                    b = st.b0 + 3 * d + 4
                    split(b, b % RING)
                    split(b + 1, (b + 1) % RING)
                    if st.upd + 1 < norms:
                        act.wait_ge(acc_free, st.o0 + d + 1)
                        square_and_round(st.upd + 1, d)
                    split(b + 2, (b + 2) % RING)

            def out_proj(st):
                for d in range(KD):
                    b = st.b0 + d + 4
                    if d < KD - 1:
                        split(b, b % RING)
                    act.wait_ge(acc_free, st.o0 + d + 1)
                    square_and_round(st.upd + 1, d)
                split(b, b % RING)

            def nat(st):
                ps = parts[st.mixer, st.j]
                for c in range(6 if st.mixer == "nsa" else 5):
                    n = NG if st.mixer == "nsa" and c == 5 else CHUNK
                    if c == 0:
                        stats(st.norm)
                    if c == TURN_CHUNK[st.mixer]:
                        turn_heads(st, range(0, 4, 2))
                    for q in range(4):
                        split(st.b0 + 4 * c + 4 + q, q)
                        for i, part in enumerate(ps):
                            if part.chunk == c - 1 and q == 0:
                                head_norm(st, i, part)
                        if st.mixer == "nsa" and c == 4 and q == 1:
                            round_windows()
                    if c == 0:
                        act.wait_ge(rstd_ready, st.norm + 1)
                    if n == NG:
                        continue
                    act.wait_ge(blocks_used, st.b0 + 4 * c + 4)
                    evacuate(st, c, n)

            def evacuate(st, c, n=CHUNK):
                for tt in range(TT):
                    if st.mixer == "nsa" and c == 0:
                        src = PS[:, tt, :].rearrange("p (g d) -> p g d", d=HD).unsqueeze(2).to_broadcast([P, 8, 2, HD])
                        nc.scalar.activation(KVD[:, tt, :, :, :], src, ACT.Copy,
                                             scale=rstd[:, tt:tt + 1]).then_inc(acc_free, 1)
                        continue
                    nc.scalar.activation(QKV[:, tt, c * CHUNK:c * CHUNK + n], PS[:, 2 * (c % 2) + tt, 0:n],
                                         ACT.Copy, scale=rstd[:, tt:tt + 1]).then_inc(acc_free, 1)

            def head_norm(st, i, part):
                act.wait_ge(heads_summed, 8 * st.nat + 2 * i + 2)
                cut = slice(part.slot, part.slot + part.heads)
                nc.scalar.activation(sdh[:, :, cut], ssh[:, :, cut], ACT.Sqrt, scale=1.0 / HD,
                                     bias=eps[:, 0:1]).then_inc(head_sd, 1)

            def turn_heads(st, banks):
                for q in banks:
                    act.wait_ge(turned, 8 * st.nat + q + 1)
                    if q == 4:
                        act.wait_ge(keys_zeroed, 2 * (st.nat + 1))
                    for dst, src in turned_tiles(st.mixer, q):
                        nc.scalar.copy(dst, src).then_inc(turned_act, 1)

            def attend(st):
                for n in range(st.branches + 2):
                    if st.mixer == "nsa":
                        compressed_step(n)
                    elif 2 <= n <= 5:
                        split(st.b0 + 22 + n, n - 2)
                    elif n == 6:
                        act.wait_ge(blocks_used, st.b0 + 24)
                        evacuate(st, 5)
                    if n >= 2:
                        m, a = n - 2, st.branch + n - 2
                        act.wait_ge(pt_full, a + 1)
                        reach(act, o_full, a - 1)
                        nc.scalar.copy(PT[:, m % 2, :], PS[:, 6 + m % 2, 0:3 * P]).then_inc(pt_ready, 1)
                    if n < st.branches:
                        a = st.branch + n
                        act.wait_ge(negmax, a + 1)
                        reach(act, pt_full, a - 1)
                        sm, pr = SM[:, n % 2, :], PR[:, n % 2, :]
                        nc.scalar.activation(pr[:, 0:P], sm[:, 0:P], ACT.Exp, scale=SCALE, bias=nm[:, n % SLOTS, 0:1],
                                             accum_out=sums[:, n % SLOTS, 0:1])
                        nc.scalar.activation(pr[:, P:3 * P], sm[:, P:3 * P], ACT.Exp, scale=SCALE,
                                             bias=nm[:, n % SLOTS, 1:2],
                                             accum_out=sums[:, n % SLOTS, 1:2]).then_inc(probs_ready, 1)

            def turn_out(st):
                for q in range(4):
                    act.wait_ge(ot_full, 4 * st.nat + q + 1)
                    nc.scalar.copy(H[:, 2 * q:2 * q + 2, 0:S], PS[:, 4 + q, :].rearrange("p (a s) -> p a s", a=2)
                                   ).then_inc(yhi_ready, 1)

            def gates_nsa(st):
                act.wait_ge(acc_free, st.o0)
                nc.scalar.activation(G[:, :, :], G[:, :, :], ACT.Sigmoid).then_inc(gate_ready, 1)

            def round_windows():
                for kv in range(2):
                    act.wait_ge(win_ready, 4 * kv + 4)
                    nc.scalar.copy(X2[:, kv, :, 0:CN], x2f[:, kv, :, :]).then_inc(win_hi, 1)

            def compress(st):
                for kv in range(2):
                    for q in range(4):
                        b = st.b0 + 4 + 4 * kv + q
                        split(b, b % RING)
                        if kv == 1 and q == 1:
                            copy_hidden(0)
                        if kv == 1 and q == 2:
                            act.wait_ge(kc_full, 1)
                            nc.scalar.activation(sqc[:, 0, :], PS[:, 4, 0:CN], ACT.Square).then_inc(kc_squared, 1)
                    if kv == 0:
                        hidden(st, 0)
                hidden(st, 1)
                act.wait_ge(kc_summed, 1)
                nc.scalar.activation(sqc[:, 1, :], PS[:, 5, 0:CN], ACT.Sqrt, scale=1.0 / HD,
                                     bias=eps[:, 0:1]).then_inc(kc_sd, 1)
                copy_hidden(1)

            def hidden(st, kv):
                act.wait_ge(blocks_used, st.b0 + 4 * kv + 4)
                nc.scalar.activation(hct[0:CN, kv, :], PS[0:CN, kv, 0:CMP_HID], ACT.Gelu_apprx_tanh
                                     ).then_inc(hidden_ready, 1)

            def copy_hidden(kv):
                act.wait_ge(hidden_turned, kv + 1)
                nc.scalar.copy(hc[:, kv, :, :], PS[:, 6 + kv, 0:2 * CN].rearrange("p (h n) -> p h n", h=2)
                               ).then_inc(hidden_copied, 1)

            def compressed_step(n):
                if n == CMP_VALUES[-1] + 1:
                    act.wait_ge(vc_full, 2)
                    nc.scalar.copy(VC[:, :, :], PS[:, 3, 256:512].rearrange("p (g d) -> p g d", g=GROUPS)
                                   ).then_inc(vc_ready, 1)
                elif n == CMP_EXP:
                    act.wait_ge(sc_step, 3)
                    nc.scalar.activation(PCE[:, :, :, 0:NCMP].rearrange("p t h n -> p (t h) n"),
                                         SC[:, :, :, 0:NCMP].rearrange("p t h n -> p (t h) n"),
                                         ACT.Exp, scale=SCALE).then_inc(pce_ready, 1)
                elif n in CMP_COPY:
                    tt = n - CMP_COPY[0]
                    act.wait_ge(pct_full, tt + 1)
                    nc.scalar.copy(PCT[:, tt, :], PS[:, 2 + tt, :]).then_inc(pct_ready, 1)

            def lambda_exp():
                act.wait_ge(consts_loaded, CONSTS * 16)
                nc.scalar.activation(lam[:, 0, :], cols[:, :, LAM], ACT.Abs).then_inc(lam_exp, 1)
                act.wait_ge(lam_exp, 1)
                nc.scalar.activation(lam[:, 1, :], lam[:, 0, :], ACT.Exp, scale=-1.0).then_inc(lam_exp, 1)

            def lru_in(st):
                for i in range(KD + 1):
                    par, b = i % 2, st.b0 + 2 * i
                    if i < KD:
                        split(b + 4, 2 * par)
                        if i == 0:
                            stats(st.norm)
                        act.wait_ge(acc_free, st.o0 + 2 * i)
                        copy_low(st, i, par, b + 2)
                    if i >= 2:
                        round_convolved(i - 2)
                    if i < KD:
                        split(b + 5, 2 * par + 1)
                    if 1 <= i <= KD:
                        act.wait_ge(lru_scaled, i)
                        nc.scalar.activation(YG[:, i - 1, :], gu[:, (i - 1) % 2, :], ACT.Gelu_apprx_tanh
                                             ).then_inc(gelu_done, 1)

            def round_convolved(i):
                act.wait_ge(tap_added, CONV * (i + 1))
                nc.scalar.copy(H[:, i, 0:S], XC[:, i, :]).then_inc(xc_hi, 1)

            def gates(st):
                for i in range(KD):
                    if i == 2:
                        round_convolved(KD - 1)
                    bank = 2 * (i % 4)
                    if i % 2 == 0:
                        act.wait_ge(gate_sums, i // 2 + 1)
                    else:
                        act.wait_ge(blocks_used, st.b0 + i // 2 + 1)
                    nc.scalar.activation(RG[:, i, :], PS[:, bank, 0:S], ACT.Sigmoid, bias=cols[:, i, BA:BA + 1])
                    nc.scalar.activation(IG[:, i, :], PS[:, bank + 1, 0:S], ACT.Sigmoid,
                                         bias=cols[:, i, BX:BX + 1]).then_inc(gates_ready, 1)
                    if i % 2 == 1 and i // 2 < 2:
                        b = st.b0 + 4 + i // 2
                        split(b, b % RING)
                for i in range(0, KD, 2):
                    act.wait_ge(log_ready, i + 2)
                    nc.scalar.activation(AA[:, i:i + 2, :], RG[:, i:i + 2, :], ACT.Exp)
                    nc.scalar.activation(TH[:, i:i + 2, :], RG[:, i:i + 2, :], ACT.Tanh).then_inc(decay_ready, 2)
                for i in range(KD):
                    act.wait_ge(mult2_ready, i + 1)
                    nc.scalar.activation(RG[:, i, :], TH[:, i, :], ACT.Sqrt, scale=-1.0).then_inc(mult_ready, 1)
                for i in range(KD):
                    act.wait_ge(hy_ready, i + 1)
                    nc.scalar.copy(H[:, i, 0:S], TH[:, i, :]).then_inc(hy_hi, 1)

            act.wait_ge(eps_set, 2)
            nc.scalar.activation(sd[:, 0:1], eps[:, 0:1], ACT.Square)
            for half in range(2):
                act.wait_ge(x_loaded[half], (32, 16)[half])
                for d in range(half * KD // 2, (half + 1) * KD // 2):
                    square_and_round(0, d)
                if half == 0:
                    split(0, 0)
            for b in range(1, RING):
                split(b, b)
            for st in stages:
                if st.kind == "up":
                    up(st)
                elif st.kind == "down":
                    down(st)
                elif st.kind == "out":
                    out_proj(st)
                elif st.kind == "nat":
                    nat(st)
                    if st.mixer == "moba":
                        turn_heads(st, range(4, 8, 2))
                        attend(st)
                        turn_out(st)
                elif st.kind == "lru_in":
                    lru_in(st)
                elif st.kind == "gates":
                    gates(st)
                elif st.kind == "compress":
                    compress(st)
                    gates_nsa(st)
                    turn_heads(st.nat_stage, range(4, 8, 2))
                    attend(st.nat_stage)
                    turn_out(st.nat_stage)

        @block.vector
        def _(dve):
            def split(b, ring, n=None):
                if isinstance(b, int):
                    if b >= n_blocks:
                        return
                    n = conv_cols(b)
                dve.wait_ge(hi_ready, b + 1)
                nc.vector.tensor_tensor(w_lo[:, ring, 0:n], raw[:, ring, 0:n], w_hi[:, ring, 0:n].bitcast(F32),
                                        ALU.subtract).then_inc(lo_ready, 1)

            def low_x(norm, d):
                dve.wait_ge(xhi_ready, norm * KD + d + 1)
                nc.vector.scalar_tensor_tensor(out=X[:, d, S:2 * S], in0=h[:, d, :], scalar=gains[:, norm, d:d + 1],
                                               in1=X[:, d, 0:S].bitcast(F32), op0=ALU.mult, op1=ALU.subtract
                                               ).then_inc(x_ready, 1)

            def update(st, d, used, c):
                dve.wait_ge(blocks_used, used)
                o, bank = st.o0 + d, d % 4
                nc.vector.scalar_tensor_tensor(out=h[:, d, :], in0=PS[:, bank, S:2 * S], scalar=c, in1=h[:, d, :],
                                               op0=ALU.mult, op1=ALU.add).then_inc(half_added, 1)
                dve.wait_ge(half_added, KD * st.upd + d + 1)
                nc.vector.scalar_tensor_tensor(out=h[:, d, :], in0=PS[:, bank, 0:S], scalar=c, in1=h[:, d, :],
                                               op0=ALU.mult, op1=ALU.add).then_inc(acc_free, 1)

            def stats(norm, nb=None):
                dve.wait_ge(sd_ready, norm + 1)
                nc.vector.reciprocal(rstd[:, :], sd[:, :]).then_inc(rstd_ready, 1)
                if nb is not None:
                    dve.wait_ge(rstd_ready, norm + 1)
                    nc.vector.tensor_tensor(rdiag[:, :, :], ident[:, :].unsqueeze(1).to_broadcast([P, TT, P]),
                                            rstd[:, :].unsqueeze(2).to_broadcast([P, TT, P]),
                                            ALU.mult).then_inc(diag_ready, 1)

            def spread(nb):
                dve.wait_ge(rb_full, nb + 1)
                nc.vector.tensor_copy(rb[:, :], PS[:, STAT, 256:512]).then_inc(rb_ready, 1)

            def add_low(st, i, par):
                dve.wait_ge(low_copied, st.pair + i + 1)
                nc.vector.tensor_tensor(pre[:, :, :], PS[:, 2 * par:2 * par + 2, 0:S], bt[:, :, :],
                                        ALU.add).then_inc(acc_free, 2)

            def low_hidden(st, i):
                dve.wait_ge(hhi_ready, NF * st.ffn + i + 1)
                nc.vector.tensor_tensor(H[:, i, S:2 * S], hf[:, :], H[:, i, 0:S].bitcast(F32),
                                        ALU.subtract).then_inc(h_ready, 1)

            def up_step(st, i, par, dyn=False, first=False):
                b = st.b0 + 2 * i
                n = dict(n=BW) if dyn else {}
                split(b + 4, 2 * par, **n)
                if first:
                    stats(st.norm, st.bcast)
                add_low(st, i, par)
                if not first:
                    low_hidden(st, i - 1)
                split(b + 5, 2 * par + 1, **n)
                if first:
                    spread(st.bcast)
                dve.wait_ge(silu_ready, NF * st.ffn + i + 1)
                if not first:
                    dve.wait_ge(h_ready, NF * st.ffn + i)
                nc.vector.tensor_tensor(hf[:, :], sg[:, :], gu[:, 1, :], ALU.mult).then_inc(prod_ready, 1)

            def up(st):
                up_step(st, 0, 0, first=True)
                up_step(st, 1, 1)
                with nc.vector.Fori(1, NF // 2 - 1) as it:
                    for s in range(2):
                        up_step(st, 2 * it + s, s, dyn=True)
                for i in (NF - 2, NF - 1):
                    up_step(st, i, i % 2)
                low_hidden(st, NF - 1)

            def down(st):
                for d in range(KD):
                    if st.mixer == "lru" and d == 2:
                        softplus()
                    b = st.b0 + 3 * d + 4
                    split(b, b % RING)
                    split(b + 1, (b + 1) % RING)
                    update(st, d, st.b0 + 3 * d + 3, 0.5)
                    if st.upd + 1 < norms:
                        low_x(st.upd + 1, d)
                    split(b + 2, (b + 2) % RING)

            def out_proj(st):
                for d in range(KD):
                    b = st.b0 + d + 4
                    update(st, d, st.b0 + d + 1, 1.0)
                    if d < KD - 1:
                        split(b, b % RING)
                    low_x(st.upd + 1, d)
                split(b, b % RING)

            def nat(st):
                ps = parts[st.mixer, st.j]
                for c in range(6 if st.mixer == "nsa" else 5):
                    if c == 0:
                        stats(st.norm)
                    if st.mixer == "nsa" and c == 4:
                        windows()
                    if st.mixer == "nsa" and c == 5:
                        low_windows()
                    if c == TURN_CHUNK[st.mixer]:
                        turn_heads(st, range(1, 4, 2))
                    for q in range(4):
                        if q == 1:
                            for i, part in enumerate(ps):
                                if part.chunk == c - 1:
                                    scale_heads(st, i, part)
                        split(st.b0 + 4 * c + 4 + q, q)
                        for i, part in enumerate(ps):
                            for tt in range(TT if part.chunk == c - 1 and q == 0 else 0):
                                n = 8 * st.nat + 2 * i + tt + 1
                                dve.wait_ge(heads_squared, n)
                                nc.vector.tensor_reduce(
                                    ssh[:, tt, part.slot:part.slot + part.heads],
                                    sqh[:, n % 2, 0:part.heads * HD].rearrange("p (a b) -> p a b", b=HD),
                                    AX.X, ALU.add).then_inc(heads_summed, 1)
                if st.mixer == "nsa":
                    nsa_gate(st)

            def scale_heads(st, i, part):
                cut = slice(part.slot, part.slot + part.heads)
                dve.wait_ge(head_sd, 4 * st.nat + i + 1)
                nc.vector.reciprocal(rqh[:, :, cut], sdh[:, :, cut]).then_inc(head_rms, 1)
                dve.wait_ge(head_rms, 4 * st.nat + i + 1)
                for tt in range(TT):
                    x = QKV[:, tt, part.col:part.col + part.heads * HD].rearrange("p (a b) -> p a b", b=HD)
                    nc.vector.tensor_tensor(x, x, rqh[:, tt, cut].unsqueeze(2).to_broadcast([P, part.heads, HD]),
                                            ALU.mult).then_inc(heads_scaled, 1)

            def turn_heads(st, banks):
                for q in banks:
                    dve.wait_ge(turned, 8 * st.nat + q + 1)
                    if q == 5:
                        dve.wait_ge(keys_zeroed, 2 * (st.nat + 1))
                    for dst, src in turned_tiles(st.mixer, q):
                        nc.vector.tensor_copy(dst, src).then_inc(turned_dve, 1)

            def attend(st):
                for n in range(st.branches + 4):
                    if st.mixer == "nsa":
                        compressed_step(st, n)
                    elif 3 <= n <= 6:
                        split(st.b0 + 21 + n, n - 3)
                    if n < st.branches:
                        a = st.branch + n
                        s = PS[:, 4 + n % 2, :]
                        dve.wait_ge(scores_full, a + 1)
                        reach(dve, probs_ready, a - 1)
                        nc.vector.tensor_tensor_reduce(SM[:, n % 2, 0:P], s[:, 0:P], tri[:, 0, :], 1.0, -3e38,
                                                       ALU.add, ALU.max, mx[:, n % SLOTS, 0:1])
                        nc.vector.tensor_tensor_reduce(SM[:, n % 2, P:3 * P], s[:, P:3 * P],
                                                       tri[:, 1:3, :].rearrange("p a b -> p (a b)"), 1.0, -3e38,
                                                       ALU.add, ALU.max, mx[:, n % SLOTS, 1:2]).then_inc(masked, 1)
                        dve.wait_ge(masked, a + 1)
                        nc.vector.tensor_scalar(nm[:, n % SLOTS, :], mx[:, n % SLOTS, :], -SCALE, None,
                                                ALU.mult).then_inc(negmax, 1)
                    if 1 <= n <= st.branches:
                        m, a = n - 1, st.branch + n - 1
                        dve.wait_ge(probs_ready, a + 1)
                        nc.vector.reciprocal(rsum[:, m % SLOTS, :], sums[:, m % SLOTS, :]).then_inc(sum_inv, 1)
                        head, _, _, gate = branch_of(st.mixer, m)
                        if gate is not None:
                            dve.wait_ge(sum_inv, a + 1)
                            nc.vector.tensor_tensor(cf[:, m % SLOTS, :], rsum[:, m % SLOTS, :],
                                                    G[:, :, 3 * head + gate], ALU.mult).then_inc(coef_ready, 1)
                    if n >= 4:
                        m, a = n - 4, st.branch + n - 4
                        head, _, _, gate = branch_of(st.mixer, m)
                        dve.wait_ge(o_full, a + 1)
                        dve.wait_ge(sum_inv, a + 1)
                        ps = PS[:, m % 2, 0:2 * HD].rearrange("p (t d) -> p t d", t=TT)
                        if gate is not None:
                            dve.wait_ge(coef_ready, m + 1)
                        if m < HEADS:
                            c = rsum if gate is None else cf
                            nc.vector.tensor_tensor(O[:, :, head * HD:(head + 1) * HD], ps,
                                                    c[:, m % SLOTS, :].unsqueeze(2).to_broadcast([P, TT, HD]),
                                                    ALU.mult).then_inc(o_done, 1)
                        else:
                            dve.wait_ge(o_done, a - HEADS + 1)
                            reach(dve, oc_done, sum(n >= at for at in CMP_ADD))
                            for tt in range(TT):
                                out = O[:, tt, head * HD:(head + 1) * HD]
                                last = nc.vector.scalar_tensor_tensor(out=out, in0=ps[:, tt, :],
                                                                      scalar=cf[:, m % SLOTS, tt:tt + 1], in1=out,
                                                                      op0=ALU.mult, op1=ALU.add)
                            last.then_inc(o_done, 1)

            def turn_out(st):
                for q in range(4):
                    dve.wait_ge(yhi_ready, 4 * st.nat + q + 1)
                    nc.vector.tensor_tensor(H[:, 2 * q:2 * q + 2, S:2 * S],
                                            PS[:, 4 + q, :].rearrange("p (a s) -> p a s", a=2),
                                            H[:, 2 * q:2 * q + 2, 0:S].bitcast(F32), ALU.subtract).then_inc(y_ready, 2)

            def nsa_gate(st):
                for tt in range(TT):
                    dve.wait_ge(blocks_used, st.b0 + st.n_blocks)
                    dve.wait_ge(acc_free, st.o0 + 10 + tt)
                    nc.vector.scalar_tensor_tensor(out=G[:, tt, :], in0=PS[:, 2 + tt, 0:NG], scalar=rstd[:, tt:tt + 1],
                                                   in1=gbias[:, :], op0=ALU.mult, op1=ALU.add).then_inc(acc_free, 1)

            def windows():
                dve.wait_ge(consts_loaded, 16 * CONSTS)
                dve.wait_ge(win_turned, 2)
                for kv in range(2):
                    for half in range(2):
                        rows = slice(half * HD, half * HD + HD)
                        v = PS[rows, 4 + 2 * kv:6 + 2 * kv, :].rearrange("p b (g n m e) -> p e m (b g) n",
                                                                         g=2, m=8, e=2)
                        for late in range(2):
                            src = v[:, half, :, :, late:late + NCMP]
                            dst = x2f[rows, kv, 8 * late:8 * late + 8, :].rearrange("p m (g n) -> p m g n", g=GROUPS)
                            add = pos[rows, kv, 8 * late:8 * late + 8].unsqueeze(2).unsqueeze(3).to_broadcast(
                                [HD, 8, GROUPS, NCMP])
                            nc.vector.tensor_tensor(dst, src, add, ALU.add).then_inc(win_ready, 1)

            def low_windows():
                for kv in range(2):
                    dve.wait_ge(win_hi, kv + 1)
                    nc.vector.tensor_tensor(X2[:, kv, :, CN:2 * CN], x2f[:, kv, :, :],
                                            X2[:, kv, :, 0:CN].bitcast(F32), ALU.subtract).then_inc(win_low, 1)

            def compress(st):
                for kv in range(2):
                    for q in range(4):
                        b = st.b0 + 4 + 4 * kv + q
                        split(b, b % RING)
                compressed_keys()

            def compressed_keys():
                dve.wait_ge(kc_sd, 1)
                nc.vector.reciprocal(sqc[:, 2, :], sqc[:, 1, :]).then_inc(kc_inv, 1)
                dve.wait_ge(kc_inv, 1)
                for e in range(2):
                    rows = slice(e * HD, (e + 1) * HD)
                    kc, inv = (x.rearrange("p (g n) -> p g n", g=GROUPS) for x in (PS[rows, 4, 0:CN], sqc[rows, 2, :]))
                    nc.vector.scalar_tensor_tensor(out=KCP[rows, :, e, 0:NCMP], in0=kc, scalar=kcgain[rows, 0:1],
                                                   in1=inv, op0=ALU.mult, op1=ALU.mult).then_inc(kc_ready, 1)

            def compressed_step(st, n):
                sc, pce, pc = (x[:, :, :, 0:NCMP] for x in (SC, PCE, PC))
                stat = (lambda i: cst[:, i, :].rearrange("p (t h) -> p t h", t=TT))
                wide = [P, TT, HEADS, NCMP]
                if n == CMP_MAX:
                    dve.wait_ge(sc_full, 4)
                    raw_sc = PS[:, 2, :].rearrange("p (t h n) -> p t h n", t=TT, h=HEADS)[:, :, :, 0:NCMP]
                    nc.vector.tensor_tensor(sc, raw_sc, cmask[:, 0, :, :].unsqueeze(2).to_broadcast(wide),
                                            ALU.add).then_inc(sc_step, 1)
                elif n == CMP_MAX + 1:
                    dve.wait_ge(sc_step, 1)
                    nc.vector.tensor_reduce(stat(0), sc, AX.X, ALU.max).then_inc(sc_step, 1)
                elif n == CMP_MAX + 2:
                    dve.wait_ge(sc_step, 2)
                    nc.vector.tensor_tensor(sc, sc, stat(0).unsqueeze(3).to_broadcast(wide),
                                            ALU.subtract).then_inc(sc_step, 1)
                elif n == CMP_SUM:
                    dve.wait_ge(pce_ready, 1)
                    nc.vector.tensor_reduce(stat(1), pce, AX.X, ALU.add).then_inc(sc_step, 1)
                elif n == CMP_SUM + 1:
                    dve.wait_ge(sc_step, 4)
                    nc.vector.reciprocal(cst[:, 2, :], cst[:, 1, :]).then_inc(sc_step, 1)
                    dve.wait_ge(sc_step, 5)
                    nc.vector.tensor_tensor(stat(3), stat(2),
                                            G[:, :, :].rearrange("p t (h b) -> p b t h", b=3)[:, 0, :, :],
                                            ALU.mult).then_inc(sc_step, 1)
                elif n == CMP_SUM + 2:
                    dve.wait_ge(sc_step, 6)
                    nc.vector.tensor_tensor(sc, pce, stat(3).unsqueeze(3).to_broadcast(wide),
                                            ALU.mult).then_inc(sc_step, 1)
                elif n == CMP_SUM + 3:
                    dve.wait_ge(sc_step, 7)
                    dve.wait_ge(nsa_zeroed, 2)
                    nc.vector.tensor_tensor(pc, sc, cmask[:, 1, :, :].unsqueeze(2).to_broadcast(wide),
                                            ALU.mult).then_inc(pc_ready, 1)
                elif n in CMP_ADD:
                    tt, half = divmod(CMP_ADD.index(n), 2)
                    dve.wait_ge(oc_full, 2 * tt + half + 1)
                    dve.wait_ge(o_done, st.branch + n - 4)
                    dst = O[:, tt, half * 512:(half + 1) * 512]
                    nc.vector.tensor_tensor(dst, PS[:, 2 + half, :], dst, ALU.add).then_inc(oc_done, 1)

            def softplus():
                def step(ins):
                    step.n += 1
                    ins.then_inc(lam_step, 1)
                    dve.wait_ge(lam_step, step.n)
                step.n = 0
                u, z, z2, p, m, r = (lam[:, n, :] for n in range(1, 7))
                v = nc.vector
                dve.wait_ge(consts_loaded, CONSTS * 16)
                dve.wait_ge(lam_exp, 2)
                step(v.tensor_scalar(m, cols[:, :, LAM], -1.0, 0.0, ALU.mult, ALU.max))
                step(v.tensor_scalar(z2, u, 2.0, None, ALU.add))
                step(v.reciprocal(r, z2))
                step(v.tensor_tensor(z, u, r, ALU.mult))
                step(v.tensor_tensor(z2, z, z, ALU.mult))
                step(v.tensor_scalar(p, z2, 1.0 / 15, None, ALU.mult))
                for n in (13, 11, 9, 7, 5, 3):
                    step(v.scalar_tensor_tensor(out=p, in0=p, scalar=1.0 / n, in1=z2, op0=ALU.add, op1=ALU.mult))
                step(v.scalar_tensor_tensor(out=p, in0=p, scalar=1.0, in1=z, op0=ALU.add, op1=ALU.mult))
                step(v.scalar_tensor_tensor(out=p, in0=p, scalar=2.0, in1=m, op0=ALU.mult, op1=ALU.add))
                step(v.tensor_scalar(loga[:, :], p, -LRU_C, None, ALU.mult))
                assert step.n == LAM_STEPS

            def lru_in(st):
                for i in range(KD + 2):
                    if i < KD:
                        par, b = i % 2, st.b0 + 2 * i
                        split(b + 4, 2 * par)
                        if i == 0:
                            stats(st.norm, st.bcast)
                        reach(dve, lru_scaled, i)
                        add_low(st, i, par)
                        split(b + 5, 2 * par + 1)
                        if i == 0:
                            spread(st.bcast)
                    if 1 <= i <= KD:
                        convolve(i - 1)
                    if i >= 2:
                        dve.wait_ge(xc_hi, i - 1)
                        nc.vector.tensor_tensor(H[:, i - 2, S:2 * S], XC[:, i - 2, :],
                                                H[:, i - 2, 0:S].bitcast(F32), ALU.subtract).then_inc(y_ready, 1)

            def convolve(i):
                dve.wait_ge(lru_scaled, i + 1)
                nc.vector.tensor_scalar(XC[:, i, :], xpad[:, i, CONV - 1:], cols[:, i, CONV - 1:CONV],
                                        cols[:, i, CONV_B:CONV_B + 1], ALU.mult, ALU.add).then_inc(tap_added, 1)
                for n in range(1, CONV):
                    dve.wait_ge(tap_added, CONV * i + n)
                    tap = CONV - 1 - n
                    nc.vector.scalar_tensor_tensor(out=XC[:, i, :], in0=xpad[:, i, tap:tap + S],
                                                   scalar=cols[:, i, tap:tap + 1], in1=XC[:, i, :],
                                                   op0=ALU.mult, op1=ALU.add).then_inc(tap_added, 1)

            def gates(st):
                dve.wait_ge(lam_step, LAM_STEPS)
                for i in range(KD):
                    dve.wait_ge(gates_ready, i + 1)
                    nc.vector.tensor_scalar(RG[:, i, :], RG[:, i, :], loga[:, i:i + 1], None, ALU.mult
                                            ).then_inc(log_ready, 1)
                    if i % 2 == 1:
                        b = st.b0 + 4 + i // 2
                        if i // 2 >= 2:
                            dve.wait_ge(block_loaded[b % RING], 16 * (b // RING + 1))
                            dve.wait_ge(blocks_used, b - RING + 1)
                            dve.wait_ge(hi_ready, b)
                            nc.vector.tensor_copy(w_hi[:, b % RING, :], raw[:, b % RING, :]).then_inc(hi_ready, 1)
                        split(b, b % RING)
                for i in range(KD):
                    dve.wait_ge(decay_squared, i + 1)
                    nc.vector.scalar_tensor_tensor(out=TH[:, i, 1:], in0=RG[:, i, 1:], scalar=1.0, in1=TH[:, i, 1:],
                                                   op0=ALU.add, op1=ALU.mult)
                    nc.vector.memset(TH[:, i, 0:1], -1.0).then_inc(mult2_ready, 1)
                for i in range(KD):
                    dve.wait_ge(mult_ready, i + 1)
                    dve.wait_ge(gated, i + 1)
                    nc.vector.tensor_tensor(IG[:, i, :], RG[:, i, :], IG[:, i, :], ALU.mult).then_inc(input_ready, 1)
                    dve.wait_ge(input_ready, i + 1)
                    nc.vector.tensor_tensor_scan(TH[:, i, :], AA[:, i, :], IG[:, i, :], 0.0,
                                                 ALU.mult, ALU.add).then_inc(scanned, 1)
                    if i >= 1:
                        low_hy(i - 1)
                low_hy(KD - 1)

            def low_hy(i):
                dve.wait_ge(hy_hi, i + 1)
                nc.vector.tensor_tensor(H[:, i, S:2 * S], TH[:, i, :], H[:, i, 0:S].bitcast(F32),
                                        ALU.subtract).then_inc(y_ready, 1)

            dve.wait_ge(x_loaded[0], 32)
            for d in range(KD // 2):
                low_x(0, d)
            split(0, 0)
            dve.wait_ge(x_loaded[1], 16)
            for d in range(KD // 2, KD):
                low_x(0, d)
            for b in range(1, RING):
                split(b, b)
            dve.wait_ge(masks_set, MASKS)
            for st in stages:
                if st.kind == "up":
                    up(st)
                elif st.kind == "down":
                    down(st)
                elif st.kind == "out":
                    out_proj(st)
                elif st.kind == "nat":
                    nat(st)
                    if st.mixer == "moba":
                        turn_heads(st, range(5, 8, 2))
                        attend(st)
                        turn_out(st)
                elif st.kind == "lru_in":
                    lru_in(st)
                elif st.kind == "gates":
                    gates(st)
                elif st.kind == "compress":
                    compress(st)
                    turn_heads(st.nat_stage, range(5, 8, 2))
                    dve.wait_ge(gate_ready, 1)
                    attend(st.nat_stage)
                    turn_out(st.nat_stage)

        @block.gpsimd
        def _(pool):
            def sum_squares(norm):
                for d in range(KD):
                    n = KD * norm + d
                    pool.wait_ge(squared, n + 1)
                    reach(pool, summed, n)
                    if d == 0:
                        nc.gpsimd.tensor_copy(ssum[:, :], sq[:, 0, :]).then_inc(summed, 1)
                    else:
                        nc.gpsimd.tensor_tensor(ssum[:, :], ssum[:, :], sq[:, d % 2, :], ALU.add).then_inc(summed, 1)

            def scale(st, i, first=False):
                pool.wait_ge(acc_free, st.o0 + 2 * i + 2)
                if first:
                    pool.wait_ge(rb_ready, st.bcast + 1)
                nc.gpsimd.tensor_tensor(gu[:, :, :], pre[:, :, :], rb[:, :].unsqueeze(1).to_broadcast([P, 2, S]),
                                        ALU.mult).then_inc(scaled, 1)

            def compress(st):
                nc.gpsimd.memset(HV[:, :, :, :, :], 0.0).then_inc(nsa_zeroed, 1)
                pool.wait_ge(nsa_zeroed, 2)
                pool.wait_ge(hidden_copied, 2)
                for hid in range(2):
                    src = hc[:, 1, hid, :].rearrange("p (g n) -> p g n", g=GROUPS).unsqueeze(2).to_broadcast(
                        [P, GROUPS, HPG, NCMP])
                    nc.gpsimd.tensor_copy(HV[:, hid, :, :, 0:NCMP], src).then_inc(hidden_spread, 1)
                pool.wait_ge(pc_ready, 1)
                pool.wait_ge(vc_ready, 1)
                nc.gpsimd.memset(VCB, 0.0).then_inc(values_spread, 1)
                for r in range(HPG):
                    rows = slice(32 * r, 32 * r + 32)
                    pool.wait_ge(values_spread, 1 + r)
                    nc.gpsimd.tensor_copy(VCB[rows, :, :, r, :],
                                          VC[rows, :, :].rearrange("p (t g) d -> p t g d", t=2)
                                          ).then_inc(values_spread, 1)

            def nat(st):
                ps = parts[st.mixer, st.j]
                if st.mixer == "nsa":
                    pool.wait_ge(acc_free, st.o0 + 1)
                    nc.gpsimd.memset(PC[:, :, :, :], 0.0).then_inc(nsa_zeroed, 1)
                pool.wait_ge(acc_free, st.o0 + 1)
                nc.gpsimd.memset(KE[:, :, :], 0.0).then_inc(keys_zeroed, 1)
                if st.mixer == "moba":
                    nc.gpsimd.memset(KO_T["moba"], 0.0).then_inc(keys_zeroed, 1)
                for i, part in enumerate(ps):
                    square_heads(st, i, part)
                    gain_heads(st, i, part)
                if st.mixer == "nsa":
                    pool.wait_ge(turned, 8 * st.nat + 4)
                    nc.gpsimd.memset(KO_T["nsa"], 0.0).then_inc(keys_zeroed, 1)

            def square_heads(st, i, part):
                for tt in range(TT):
                    n = 8 * st.nat + 2 * i + tt + 1
                    pool.wait_ge(acc_free, st.o0 + 2 * part.chunk + 2)
                    reach(pool, heads_summed, n - 2)
                    x = QKV[:, tt, part.col:part.col + part.heads * HD]
                    nc.gpsimd.tensor_tensor(sqh[:, n % 2, 0:part.heads * HD], x, x, ALU.mult).then_inc(heads_squared, 1)

            def gain_heads(st, i, part):
                for tt in range(TT):
                    pool.wait_ge(heads_scaled, 8 * st.nat + 2 * i + tt + 1)
                    x = QKV[:, tt, part.col:part.col + part.heads * HD].rearrange("p (a b) -> p a b", b=HD)
                    g = hgain[:, part.gain, :].unsqueeze(1).to_broadcast([P, part.heads, HD])
                    if part.col in (KS_COL, KW_COL) and st.mixer == "nsa":
                        dst = (KSD if part.col == KS_COL else KWD)[:, tt]
                        for e in range(2):
                            last = nc.gpsimd.tensor_tensor(dst[:, :, e, :], x, g, ALU.mult)
                        last.then_inc(heads_gained, 1)
                    else:
                        nc.gpsimd.tensor_tensor(x, x, g, ALU.mult).then_inc(heads_gained, 1)

            def lru_in(st):
                nc.gpsimd.memset(xpad[:, :, 0:CONV - 1], 0.0).then_inc(pad_set, 1)
                for i in range(KD):
                    pool.wait_ge(acc_free, st.o0 + 2 * i + 2)
                    if i == 0:
                        pool.wait_ge(rb_ready, st.bcast + 1)
                        pool.wait_ge(pad_set, 1)
                    reach(pool, gelu_done, i - 1)
                    nc.gpsimd.tensor_tensor(xpad[:, i, CONV - 1:], pre[:, 0, :], rb[:, :], ALU.mult)
                    nc.gpsimd.tensor_tensor(gu[:, i % 2, :], pre[:, 1, :], rb[:, :], ALU.mult).then_inc(lru_scaled, 1)

            def gates(st):
                for i in range(KD):
                    pool.wait_ge(gates_ready, i + 1)
                    nc.gpsimd.tensor_tensor(IG[:, i, :], IG[:, i, :], XC[:, i, :], ALU.mult).then_inc(gated, 1)
                for i in range(KD):
                    pool.wait_ge(decay_ready, i + 1)
                    nc.gpsimd.tensor_tensor(RG[:, i, :], AA[:, i, :], AA[:, i, :], ALU.mult
                                            ).then_inc(decay_squared, 1)
                for i in range(KD):
                    pool.wait_ge(scanned, i + 1)
                    nc.gpsimd.tensor_tensor(TH[:, i, :], TH[:, i, :], YG[:, i, :], ALU.mult).then_inc(hy_ready, 1)

            nc.gpsimd.memset(eps[:, :], EPS).then_inc(eps_set, 1)
            nc.gpsimd.memset(KCP[:, :, :, :], 0.0).then_inc(eps_set, 1)
            nc.gpsimd.memset(ones[:, :], 1.0).then_inc(masks_set, 1)
            nc.gpsimd.memset(ident[:, :], 0.0).then_inc(masks_set, 1)
            nc.gpsimd.memset(tri[:, :, :], 0.0).then_inc(masks_set, 1)
            pool.wait_ge(masks_set, 3)
            nc.gpsimd.affine_select(out=ident[:, :], in_=ident[:, :], compare_op=ALU.not_equal, fill=1.0, base=0,
                                    pattern=[[-1, P]], channel_multiplier=1).then_inc(masks_set, 1)
            for a in (0, 2):
                nc.gpsimd.affine_select(out=tri[:, a, :], in_=tri[:, a, :], compare_op=ALU.is_ge, fill=NEG, base=0,
                                        pattern=[[-1, P]], channel_multiplier=1).then_inc(masks_set, 1)
            nc.gpsimd.memset(cmask[:, 0, :, :], 0.0).then_inc(masks_set, 1)
            nc.gpsimd.memset(cmask[:, 1, :, :], 1.0).then_inc(masks_set, 1)
            nc.gpsimd.memset(blk[:, :], 0.0).then_inc(masks_set, 1)
            pool.wait_ge(masks_set, 9)
            nc.gpsimd.memset(blk[0:HD, 0:HD], 1.0).then_inc(masks_set, 1)
            nc.gpsimd.memset(blk[HD:P, HD:P], 1.0).then_inc(masks_set, 1)
            pool.wait_ge(masks_set, 11)
            for m, fill in ((0, NEG), (1, 0.0)):
                nc.gpsimd.affine_select(out=cmask[:, m, :, :], in_=cmask[:, m, :, :], compare_op=ALU.is_ge, fill=fill,
                                        base=1 - CMP_L, pattern=[[P, TT], [-CMP_D, NCMP]],
                                        channel_multiplier=1).then_inc(masks_set, 1)
            sum_squares(0)
            for name, dst in const_loads:
                pool.dma_start(dst, t[name]).then_inc(consts_loaded, 16)
            pool.wait_ge(consts_loaded, 16 * CONSTS)
            for st in stages:
                if st.kind == "up":
                    scale(st, 0, first=True)
                    with nc.gpsimd.Fori(1, NF) as i:
                        scale(st, i)
                elif st.kind in ("down", "out"):
                    if st.upd + 1 < norms:
                        sum_squares(st.upd + 1)
                elif st.kind == "nat":
                    nat(st)
                elif st.kind == "lru_in":
                    lru_in(st)
                elif st.kind == "gates":
                    gates(st)
                elif st.kind == "compress":
                    compress(st)


MASKS = 13
LAM_STEPS = 15
TURNED = 6
TURN_CHUNK = {"moba": 4, "nsa": 5}
CMP_SCORES, CMP_MAX, CMP_VALUES, CMP_EXP, CMP_SUM = range(2, 6), 7, range(8, 10), 11, 13
CMP_TURN, CMP_COPY, CMP_OUT, CMP_ADD = 18, range(19, 21), (21, 22, 27, 28), (24, 25, 30, 31)
CONV_B, BA, BX, LAM = range(CONV, CONV + 4)


def branch_of(mixer, n):
    if mixer == "moba":
        return n, n // 2, MOBA_V_COL + n * HD, None
    head, gate = n % HEADS, 1 + n // HEADS
    g = head // HPG
    return head, (0 if gate == 1 else 4) + g, (VS_COL if gate == 1 else VW_COL) + g * HD, gate


def stream_layout(w, cols):
    k, n = w.shape
    return w.reshape(k // P, P, n // cols, cols).transpose(2, 1, 0, 3).reshape(n // cols, P, k // P * cols)


def layout(depth, a):
    arrays = {}
    arrays["x"] = a["x"][0].T.reshape(KD, P, S).transpose(1, 0, 2)
    arrays["norm_g"] = a["norm_g"][0:depth].reshape(3 * depth, KD, P).transpose(2, 0, 1)
    ups, downs = [], []
    for layer in range(depth):
        for which in ("ffn1", "ffn2"):
            w = a[f"{which}_wi"][layer]
            blocks = stream_layout(w, P)
            ups.append(blocks.reshape(2, NF, P, BW).transpose(1, 0, 2, 3).reshape(2 * NF, P, BW))
            downs.append(stream_layout(a[f"{which}_wo"][layer], P))
    arrays["up_w"] = np.stack(ups)
    arrays["down_w"] = np.stack(downs)

    def token_major(w):
        n = w.shape[1]
        return w.reshape(4, 2, P, n).transpose(0, 2, 1, 3).reshape(4, P, 2 * n)

    arrays["moba_w"] = np.stack([np.concatenate([token_major(w[:, c:c + CHUNK]) for c in range(0, 3072, CHUNK)])
                                 for w in a["moba_w_in"]])
    arrays["moba_o"] = np.stack([stream_layout(w, P) for w in a["moba_w_out"]])
    arrays["hgain"] = np.concatenate([a["moba_q_gain"][0], a["moba_k_gain"][0], a["nsa_q_gain"][0],
                                      a["nsa_ks_gain"][0], a["nsa_kw_gain"][0], a["moba_q_gain"][1],
                                      a["moba_k_gain"][1]]).reshape(1, 7, HD).repeat(P, 0)
    arrays["lru_w"] = np.stack([stream_layout(w, P).reshape(2, KD, P, BW).transpose(1, 0, 2, 3).reshape(2 * KD, P, BW)
                                for w in a["lru_w_in"]])
    both = np.stack([a["lru_wa"], a["lru_wx"]], 2)[:, :, :].reshape(-1, 4, 2, 2, P, 2, P)
    arrays["lru_g"] = both.transpose(0, 1, 4, 5, 2, 3, 6).reshape(-1, 4, P, BW)
    arrays["lru_o"] = np.stack([stream_layout(w, P) for w in a["lru_w_out"]])
    w = a["nsa_w_in"]
    q, kc, vc, ks, vs, kw, vw, g = np.split(w, np.cumsum([D] + [GROUPS * HD] * 6), axis=-1)
    chunks = [np.concatenate([kc, vc], -1), q[:, :, 0:CHUNK], q[:, :, CHUNK:], np.concatenate([ks, vs], -1),
              np.concatenate([kw, vw], -1)]
    arrays["nsa_w"] = np.stack([np.concatenate([token_major(c[j]) for c in chunks]) for j in range(w.shape[0])])
    arrays["nsa_g"] = np.stack([token_major(x) for x in g])
    arrays["nsa_o"] = np.stack([stream_layout(w, P) for w in a["nsa_w_out"]])
    w1 = np.stack([a["nsa_ck_w1"], a["nsa_cv_w1"]], 1).reshape(-1, 2, 4, 4, P, CMP_HID)
    arrays["nsa_c"] = w1.transpose(0, 1, 2, 4, 3, 5).reshape(-1, 8, P, BW)
    arrays["nsa_pos"] = np.stack([a["nsa_pos_k"][0], a["nsa_pos_v"][0]]).reshape(2, NPAIR, P).transpose(2, 0, 1)
    w2 = a["nsa_ck_w2"][0].reshape(2, P, HD).transpose(1, 0, 2)
    arrays["nsa_w2k"] = np.concatenate([w2, w2], -1)
    arrays["nsa_w2v"] = a["nsa_cv_w2"][0].reshape(2, P, HD).transpose(1, 0, 2)
    arrays["nsa_kc_gain"] = np.concatenate([a["nsa_kc_gain"][0]] * 2)[:, None]
    arrays["nsa_gate_b"] = a["nsa_gate_b"].repeat(P, 0)
    per_channel = [a["lru_conv_w"][0, n, 0] for n in range(CONV)] + [a[k][0] for k in
                                                                     ("lru_conv_b", "lru_ba", "lru_bx", "lru_lam")]
    arrays["lru_cols"] = np.stack(per_channel, -1).reshape(KD, P, CONV + 4).transpose(1, 0, 2)
    return {k: np.ascontiguousarray(v) for k, v in arrays.items()}


def kernel(**inputs):
    import concourse.bacc as bacc
    from concourse.bass_utils import run_bass_kernel_spmd

    arrays = layout(DEPTH, {k: np.asarray(v) for k, v in inputs.items()})
    nc = bacc.Bacc("TRN2", target_bir_lowering=False, num_devices=1)
    t = {k: nc.dram_tensor(f"in_{k}", v.shape, mybir.dt.from_np(v.dtype), kind="ExternalInput").ap()
         for k, v in arrays.items()}
    t["out"] = nc.dram_tensor("out", (P, KD, S), F32, kind="ExternalOutput").ap()
    trunk_program(nc, DEPTH, t)
    r = run_bass_kernel_spmd(nc, [{f"in_{k}": v for k, v in arrays.items()}], core_ids=[0])
    got = np.asarray(r.results[0]["out"])
    return np.ascontiguousarray(got.transpose(1, 0, 2).reshape(D, S).T[None])
```
